# Optimizing a Trainium2 kernel written in Bass

```python
import math
import jax, jax.numpy as jnp
from jax import lax
import numpy as np

D_MODEL = 1024
BATCH = 1
SEQ = 128
DEPTH = 1
DEC_BATCH = 1
DEC_SEQ = 512
PAST_LEN = 128

GRID_W = 64
H_A = 8
D_HA = 64
W_A = H_A * D_HA
WIN_H = 8
WIN_W = 16
QB_W = 16
BAND_W = 2 * WIN_W
H_B = 4
D_K = 128
D_V = 128
W_B = H_B * D_V
CONV_K = 5
CHUNK = 64
ROPE_BASE = 10000.0
N_GROUPS = 4
EXP_PER_GROUP = 8
N_EXPERTS = N_GROUPS * EXP_PER_GROUP
TOP_K = 2
D_FF_E = 256
EPS = 1e-6
IN_WIDTH = 3 * W_A + 2 * H_B * D_K + 2 * W_B + 4 * H_B + 2 * D_MODEL

kernel_name = "hybrid_na_gdn_hmoe_diffusion_step"

def _in_split_points():
    sizes = (W_A, W_A, W_A, H_B * D_K, H_B * D_K, W_B, W_B, H_B, H_B, H_B, H_B, D_MODEL, D_MODEL)
    points, acc = [], 0
    for s in sizes[:-1]:
        acc += s
        points.append(acc)
    return points

def rms_norm(x, w):
    xf = x.astype(jnp.float32)
    y = xf * lax.rsqrt(jnp.mean(xf * xf, axis=-1, keepdims=True) + EPS)
    return (y * w.astype(jnp.float32)).astype(x.dtype)

def l2_norm(x):
    xf = x.astype(jnp.float32)
    return (xf * lax.rsqrt(jnp.sum(xf * xf, axis=-1, keepdims=True) + EPS)).astype(x.dtype)

def axial_rope_tables(L):
    pos = jnp.arange(L)
    rows = (pos // GRID_W).astype(jnp.float32)
    cols = (pos % GRID_W).astype(jnp.float32)
    n_pairs = D_K // 4
    inv = ROPE_BASE ** (-jnp.arange(n_pairs, dtype=jnp.float32) / n_pairs)
    ang = jnp.concatenate([rows[:, None] * inv, cols[:, None] * inv], axis=-1)
    return jnp.cos(ang), jnp.sin(ang)

def apply_rope(x, cos, sin):
    xf = x.astype(jnp.float32).reshape(x.shape[:-1] + (x.shape[-1] // 2, 2))
    x1, x2 = xf[..., 0], xf[..., 1]
    c = cos[None, :, None, :]
    s = sin[None, :, None, :]
    out = jnp.stack([x1 * c - x2 * s, x1 * s + x2 * c], axis=-1).reshape(x.shape)
    return out.astype(x.dtype)

def short_conv(x, w):
    C = x.shape[-1]
    y = lax.conv_general_dilated(x, w[:, None, :].astype(x.dtype), window_strides=(1,),
                                 padding=[(CONV_K // 2, CONV_K // 2)],
                                 dimension_numbers=('NWC', 'WIO', 'NWC'),
                                 feature_group_count=C)
    return jax.nn.silu(y)

def context_attention(q, k, v):
    s = jnp.einsum('bqhd,bkhd->bhqk', q, k).astype(jnp.float32) * (q.shape[-1] ** -0.5)
    p = jax.nn.softmax(s, axis=-1).astype(v.dtype)
    return jnp.einsum('bhqk,bkhd->bqhd', p, v)

def neighbourhood_attention(q, k, v, k_ctx, v_ctx, rpb):
    B, L, H, D = q.shape
    rows = L // GRID_W
    kh = min(WIN_H, rows)
    n_cb = GRID_W // QB_W
    n_keys = kh * BAND_W
    r = jnp.arange(rows)
    key_rows = jnp.clip(r - kh // 2, 0, rows - kh)[:, None] + jnp.arange(kh)[None, :]
    m = jnp.arange(n_cb)
    key_cols = (jnp.clip(m * QB_W - WIN_W // 2, 0, GRID_W - BAND_W)[:, None]
                + jnp.arange(BAND_W)[None, :])
    q_cols = m[:, None] * QB_W + jnp.arange(QB_W)[None, :]
    win_start = jnp.clip(q_cols - WIN_W // 2, 0, GRID_W - WIN_W)
    kg = k.reshape(B, rows, GRID_W, H, D)
    vg = v.reshape(B, rows, GRID_W, H, D)
    ridx = key_rows[:, None, :, None]
    cidx = key_cols[None, :, None, :]
    k_band = kg[:, ridx, cidx].reshape(B, rows, n_cb, n_keys, H, D)
    v_band = vg[:, ridx, cidx].reshape(B, rows, n_cb, n_keys, H, D)
    qg = q.reshape(B, rows, n_cb, QB_W, H, D)
    scale = D ** -0.5
    s_loc = jnp.einsum('brmqhd,brmkhd->bhrmqk', qg, k_band).astype(jnp.float32) * scale
    kc = key_cols[:, None, :]
    ws = win_start[:, :, None]
    in_win = (kc >= ws) & (kc < ws + WIN_W)
    mask = jnp.broadcast_to(in_win[:, :, None, :], (n_cb, QB_W, kh, BAND_W)).reshape(n_cb, QB_W, n_keys)
    dr = key_rows - r[:, None] + (WIN_H - 1)
    dc = jnp.clip(key_cols[:, None, :] - q_cols[:, :, None] + (WIN_W - 1), 0, 2 * WIN_W - 2)
    bias = rpb[:, dr[:, None, None, :, None], dc[None, :, :, None, :]]
    bias = bias.reshape(H, rows, n_cb, QB_W, n_keys).astype(jnp.float32)
    s_loc = jnp.where(mask, s_loc + bias, -1e30)
    s_ctx = jnp.einsum('brmqhd,bchd->bhrmqc', qg, k_ctx).astype(jnp.float32) * scale
    p = jax.nn.softmax(jnp.concatenate([s_loc, s_ctx], axis=-1), axis=-1).astype(v.dtype)
    o = (jnp.einsum('bhrmqk,brmkhd->brmqhd', p[..., :n_keys], v_band)
         + jnp.einsum('bhrmqc,bchd->brmqhd', p[..., n_keys:], v_ctx))
    return o.reshape(B, L, H, D)

def gated_delta_chunked(q, k, v, g, beta, s0):
    B, L, H, DK = q.shape
    DV = v.shape[-1]
    n = L // CHUNK
    f32 = jnp.float32

    def to_chunks(t):
        t = t.astype(f32).reshape((B, n, CHUNK, H) + t.shape[3:])
        return jnp.moveaxis(t, (1, 3), (0, 2))

    qc = to_chunks(q) * (DK ** -0.5)
    kc = to_chunks(k)
    vc = to_chunks(v)
    bc = to_chunks(beta)
    gc = jnp.cumsum(to_chunks(g), axis=-1)
    tril = jnp.tril(jnp.ones((CHUNK, CHUNK), dtype=bool))
    strict = jnp.tril(jnp.ones((CHUNK, CHUNK), dtype=bool), -1)
    diff = gc[..., :, None] - gc[..., None, :]
    decay = jnp.where(tril, jnp.exp(jnp.where(tril, diff, 0.0)), 0.0)
    kb = kc * bc[..., None]
    a_mat = jnp.where(strict, jnp.einsum('nbhik,nbhjk->nbhij', kb, kc) * decay, 0.0)
    eye = jnp.eye(CHUNK, dtype=f32)
    t_inv = lax.linalg.triangular_solve(eye + a_mat, jnp.broadcast_to(eye, a_mat.shape),
                                        left_side=True, lower=True)
    u = jnp.einsum('nbhij,nbhjv->nbhiv', t_inv, vc * bc[..., None])
    w = jnp.einsum('nbhij,nbhjk->nbhik', t_inv, kb * jnp.exp(gc)[..., None])

    def step(S, xs):
        q_i, k_i, u_i, w_i, g_i, dec_i = xs
        v_new = u_i - jnp.einsum('bhck,bhkv->bhcv', w_i, S)
        intra = jnp.einsum('bhik,bhjk->bhij', q_i, k_i) * dec_i
        o = (jnp.einsum('bhck,bhkv->bhcv', q_i * jnp.exp(g_i)[..., None], S)
             + jnp.einsum('bhij,bhjv->bhiv', intra, v_new))
        g_last = g_i[..., -1:]
        S = (S * jnp.exp(g_last)[..., None]
             + jnp.einsum('bhck,bhcv->bhkv', k_i * jnp.exp(g_last - g_i)[..., None], v_new))
        return S, o

    S, o = lax.scan(step, s0.astype(f32), (qc, kc, u, w, gc, decay))
    o = jnp.moveaxis(o, (0, 2), (1, 3)).reshape(B, L, H, DV)
    return o.astype(v.dtype), S.astype(s0.dtype)

def bidirectional_delta(q, k, v, g_f, g_b, b_f, b_b, s_f, s_b):
    o_f, S_f = gated_delta_chunked(q, k, v, g_f, b_f, s_f)
    o_b, S_b = gated_delta_chunked(q[:, ::-1], k[:, ::-1], v[:, ::-1], g_b[:, ::-1], b_b[:, ::-1], s_b)
    return o_f + o_b[:, ::-1], S_f, S_b

def log_decay(a, a_log, dt_bias):
    return -jnp.exp(a_log.astype(jnp.float32)) * jax.nn.softplus((a + dt_bias).astype(jnp.float32))

def token_mix(h, w_in, conv_w, a_log, dt_bias, q_norm_w, k_norm_w, rpb, o_norm_w,
              w_proj_a, w_proj_b, w_out, k_ctx, v_ctx, s_f, s_b):
    B, L, _ = h.shape
    qa, ka, va, qb, kb, vb, zb, a_f, a_b, b_f, b_b, ga, gb = jnp.split(h @ w_in, _in_split_points(), axis=-1)
    qa = rms_norm(qa.reshape(B, L, H_A, D_HA), q_norm_w)
    ka = rms_norm(ka.reshape(B, L, H_A, D_HA), k_norm_w)
    va = va.reshape(B, L, H_A, D_HA)
    if k_ctx is None:
        o_a = context_attention(qa, ka, va)
    else:
        o_a = neighbourhood_attention(qa, ka, va, k_ctx, v_ctx, rpb)
    qkv = short_conv(jnp.concatenate([qb, kb, vb], axis=-1), conv_w)
    qd, kd, vd = jnp.split(qkv, [H_B * D_K, 2 * H_B * D_K], axis=-1)
    qd = l2_norm(qd.reshape(B, L, H_B, D_K))
    kd = l2_norm(kd.reshape(B, L, H_B, D_K))
    if k_ctx is not None:
        cos, sin = axial_rope_tables(L)
        qd = apply_rope(qd, cos, sin)
        kd = apply_rope(kd, cos, sin)
    vd = vd.reshape(B, L, H_B, D_V)
    g_f = log_decay(a_f, a_log[0], dt_bias[0])
    g_b = log_decay(a_b, a_log[1], dt_bias[1])
    o_b, S_f, S_b = bidirectional_delta(qd, kd, vd, g_f, g_b, jax.nn.sigmoid(b_f), jax.nn.sigmoid(b_b), s_f, s_b)
    o_b = rms_norm(o_b, o_norm_w) * jax.nn.silu(zb.reshape(B, L, H_B, D_V))
    merged = (jax.nn.sigmoid(ga) * (o_a.reshape(B, L, W_A) @ w_proj_a)
              + jax.nn.sigmoid(gb) * (o_b.reshape(B, L, W_B) @ w_proj_b))
    return merged @ w_out, ka, va, S_f, S_b

def hier_moe(h, w_router_g, b_router_g, w_router_e, b_router_e, w_exp_gate, w_exp_up, w_exp_down):
    f32 = jnp.float32
    grp_logits = (h @ w_router_g).astype(f32) + b_router_g.astype(f32)
    grp = jnp.argmax(grp_logits, axis=-1)
    p_grp = jnp.max(jax.nn.softmax(grp_logits, axis=-1), axis=-1, keepdims=True)
    exp_logits = ((h @ w_router_e).astype(f32) + b_router_e.astype(f32)).reshape(
        h.shape[:-1] + (N_GROUPS, EXP_PER_GROUP))
    in_grp = jnp.take_along_axis(exp_logits, grp[..., None, None], axis=-2)[..., 0, :]
    top_p, top_i = lax.top_k(jax.nn.softmax(in_grp, axis=-1), TOP_K)
    wts = p_grp * top_p / jnp.sum(top_p, axis=-1, keepdims=True)
    ids = grp[..., None] * EXP_PER_GROUP + top_i
    combine = jnp.sum(jax.nn.one_hot(ids, N_EXPERTS, dtype=f32) * wts[..., None], axis=-2)
    hid = (jax.nn.silu(jnp.einsum('bld,edf->blef', h, w_exp_gate))
           * jnp.einsum('bld,edf->blef', h, w_exp_up))
    hid = hid * combine[..., None].astype(h.dtype)
    return jnp.einsum('blef,efd->bld', hid, w_exp_down)

def layer_forward(x, cond, norm1_w, norm2_w, w_mod, b_mod, w_in, conv_w, a_log, dt_bias,
                  q_norm_w, k_norm_w, rpb, o_norm_w, w_proj_a, w_proj_b, w_out,
                  w_router_g, b_router_g, w_router_e, b_router_e, w_exp_gate, w_exp_up, w_exp_down,
                  k_ctx, v_ctx, s_f, s_b):
    mod = (jax.nn.silu(cond) @ w_mod + b_mod)[:, None, :]
    sh1, sc1, g1, sh2, sc2, g2 = jnp.split(mod, 6, axis=-1)
    h = rms_norm(x, norm1_w) * (1.0 + sc1) + sh1
    mix, k_a, v_a, S_f, S_b = token_mix(h, w_in, conv_w, a_log, dt_bias, q_norm_w, k_norm_w, rpb,
                                        o_norm_w, w_proj_a, w_proj_b, w_out, k_ctx, v_ctx, s_f, s_b)
    x = x + g1 * mix
    h = rms_norm(x, norm2_w) * (1.0 + sc2) + sh2
    x = x + g2 * hier_moe(h, w_router_g, b_router_g, w_router_e, b_router_e, w_exp_gate, w_exp_up, w_exp_down)
    return x, k_a, v_a, S_f, S_b

def setup_inputs(seed: int = 0) -> dict:
    key = jax.random.key(seed)
    ks = jax.random.split(key, 32)
    f32 = jnp.float32

    def nrm(k, shape, scale):
        return jax.random.normal(k, shape, f32) * scale

    L = DEPTH
    dt = jnp.exp(jax.random.uniform(ks[12], (L, 2, H_B), f32, minval=math.log(1e-3), maxval=math.log(1e-1)))
    return {
        'x_prompt': nrm(ks[0], (BATCH, SEQ, D_MODEL), 1.0),
        'x_sample': nrm(ks[1], (DEC_BATCH, DEC_SEQ, D_MODEL), 1.0),
        'c': nrm(ks[2], (DEC_BATCH, D_MODEL), 1.0),
        'cache_attn_k': nrm(ks[3], (DEC_BATCH, DEPTH, PAST_LEN, H_A, D_HA), 1.0),
        'cache_attn_v': nrm(ks[4], (DEC_BATCH, DEPTH, PAST_LEN, H_A, D_HA), 1.0),
        'state_delta_fwd': nrm(ks[5], (DEC_BATCH, DEPTH, H_B, D_K, D_V), D_K ** -0.5),
        'state_delta_bwd': nrm(ks[6], (DEC_BATCH, DEPTH, H_B, D_K, D_V), D_K ** -0.5),
        'c_ctx': nrm(ks[7], (D_MODEL,), 1.0),
        'norm1_w': 1.0 + nrm(ks[8], (L, D_MODEL), 0.02),
        'norm2_w': 1.0 + nrm(ks[9], (L, D_MODEL), 0.02),
        'w_mod': nrm(ks[10], (L, D_MODEL, 6 * D_MODEL), 0.5 * D_MODEL ** -0.5),
        'b_mod': nrm(ks[11], (L, 6 * D_MODEL), 0.02),
        'w_in': nrm(ks[13], (L, D_MODEL, IN_WIDTH), D_MODEL ** -0.5),
        'conv_w': nrm(ks[14], (L, CONV_K, 2 * H_B * D_K + W_B), CONV_K ** -0.5),
        'a_log': jnp.log(jax.random.uniform(ks[15], (L, 2, H_B), f32, minval=1.0, maxval=16.0)),
        'dt_bias': dt + jnp.log(-jnp.expm1(-dt)),
        'q_norm_w': 1.0 + nrm(ks[16], (L, D_HA), 0.02),
        'k_norm_w': 1.0 + nrm(ks[17], (L, D_HA), 0.02),
        'rpb': nrm(ks[18], (L, H_A, 2 * WIN_H - 1, 2 * WIN_W - 1), 0.1),
        'o_norm_w': 1.0 + nrm(ks[19], (L, D_V), 0.02),
        'w_proj_a': nrm(ks[20], (L, W_A, D_MODEL), W_A ** -0.5),
        'w_proj_b': nrm(ks[21], (L, W_B, D_MODEL), W_B ** -0.5),
        'w_out': nrm(ks[22], (L, D_MODEL, D_MODEL), D_MODEL ** -0.5),
        'w_router_g': nrm(ks[23], (L, D_MODEL, N_GROUPS), D_MODEL ** -0.5),
        'b_router_g': nrm(ks[24], (L, N_GROUPS), 0.01),
        'w_router_e': nrm(ks[25], (L, D_MODEL, N_EXPERTS), D_MODEL ** -0.5),
        'b_router_e': nrm(ks[26], (L, N_EXPERTS), 0.01),
        'w_exp_gate': nrm(ks[27], (L, N_EXPERTS, D_MODEL, D_FF_E), D_MODEL ** -0.5),
        'w_exp_up': nrm(ks[28], (L, N_EXPERTS, D_MODEL, D_FF_E), D_MODEL ** -0.5),
        'w_exp_down': nrm(ks[29], (L, N_EXPERTS, D_FF_E, D_MODEL), D_FF_E ** -0.5),
    }

def reference(x_prompt, x_sample, c, cache_attn_k, cache_attn_v, state_delta_fwd, state_delta_bwd,
              c_ctx, norm1_w, norm2_w, w_mod, b_mod, w_in, conv_w, a_log, dt_bias,
              q_norm_w, k_norm_w, rpb, o_norm_w, w_proj_a, w_proj_b, w_out,
              w_router_g, b_router_g, w_router_e, b_router_e, w_exp_gate, w_exp_up, w_exp_down):
    y_p = x_prompt
    y_s = x_sample
    new_k, new_v, new_sf, new_sb = [], [], [], []
    for l in range(DEPTH):
        lw = dict(norm1_w=norm1_w[l], norm2_w=norm2_w[l], w_mod=w_mod[l], b_mod=b_mod[l],
                  w_in=w_in[l], conv_w=conv_w[l], a_log=a_log[l], dt_bias=dt_bias[l],
                  q_norm_w=q_norm_w[l], k_norm_w=k_norm_w[l], rpb=rpb[l], o_norm_w=o_norm_w[l],
                  w_proj_a=w_proj_a[l], w_proj_b=w_proj_b[l], w_out=w_out[l],
                  w_router_g=w_router_g[l], b_router_g=b_router_g[l],
                  w_router_e=w_router_e[l], b_router_e=b_router_e[l],
                  w_exp_gate=w_exp_gate[l], w_exp_up=w_exp_up[l], w_exp_down=w_exp_down[l])
        zeros = jnp.zeros((x_prompt.shape[0], H_B, D_K, D_V), x_prompt.dtype)
        y_p, k_a, v_a, s_f, s_b = layer_forward(y_p, c_ctx[None, :], k_ctx=None, v_ctx=None,
                                                s_f=zeros, s_b=zeros, **lw)
        new_k.append(k_a)
        new_v.append(v_a)
        new_sf.append(s_f)
        new_sb.append(s_b)
        y_s, _, _, _, _ = layer_forward(y_s, c, k_ctx=cache_attn_k[:, l], v_ctx=cache_attn_v[:, l],
                                        s_f=state_delta_fwd[:, l], s_b=state_delta_bwd[:, l], **lw)
    new_attn_k = jnp.stack(new_k, axis=1)
    new_attn_v = jnp.stack(new_v, axis=1)
    new_delta_fwd = jnp.stack(new_sf, axis=1)
    new_delta_bwd = jnp.stack(new_sb, axis=1)
    return (y_p, y_s, new_attn_k, new_attn_v, new_delta_fwd, new_delta_bwd)


_drawn_inputs = setup_inputs


def setup_inputs(seed=0):
    import zlib

    import numpy as np

    out = dict(_drawn_inputs(seed))
    spreads = {}
    factors = {'cache_attn_k': 4.43,
     'cache_attn_v': 3.585,
     'state_delta_fwd': 6.579,
     'state_delta_bwd': 6.127,
     'norm2_w': 5.126,
     'q_norm_w': 8.0,
     'k_norm_w': 2.852,
     'rpb': 24.625,
     'o_norm_w': 8.0,
     'b_router_g': 8.0,
     'b_router_e': 8.0}
    for name, (base, spread) in spreads.items():
        noise = np.random.default_rng([zlib.crc32(name.encode()), seed]).standard_normal(out[name].shape)
        drawn = base * np.exp(spread * noise) if base else spread * noise
        out[name] = __import__('jax').numpy.asarray(drawn.astype(out[name].dtype))
    for name, factor in factors.items():
        out[name] = (out[name] * factor).astype(out[name].dtype)
    return out
```

```python
from contextlib import ExitStack

import numpy as np

import concourse.bass as bass
from concourse import mybir

F32 = mybir.dt.float32
BF16 = mybir.dt.bfloat16
ALU = mybir.AluOpType
ACT = mybir.ActivationFunctionType
AX_X = mybir.AxisListType.X

P = 128
D = 1024
KC = D // P
SEQ, DEC_SEQ, PAST = 128, 512, 128
TOK = SEQ + DEC_SEQ
T = TOK // P
GRID_W, ROWS = 64, DEC_SEQ // 64
H_A, D_HA, W_A = 8, 64, 512
WIN_H, WIN_W, QB_W, BAND_W = 8, 16, 16, 32
N_CB = GRID_W // QB_W
BAND = ROWS * BAND_W
KEYS = BAND + PAST
BAND_START = [min(max(m * QB_W - WIN_W // 2, 0), GRID_W - BAND_W) for m in range(N_CB)]
BIAS_OF = [0, 1, 1, 2]
H_B, DK, W_B = 4, 128, 512
CONV_K = 5
LEVELS = [1, 2, 4, 8, 16, 32, 64]
N_GROUPS, EXP_PER_GROUP = 4, 8
N_EXPERTS = N_GROUPS * EXP_PER_GROUP
D_FF = 256
EPS = 1e-6
BIG = 1e30
HALF = 512
NHALF = D // HALF
XC = 2 + SEQ + 2 + DEC_SEQ + 2
YC = XC - CONV_K + 1

BLOCKS = (["mod0", "mod1", "mod2", "mod3", "qa", "ka", "va", "qb", "kb", "vb", "zb"]
          + [f"mod{j}" for j in range(4, 12)]
          + ["proj0", "ga0", "gb0", "proj1", "ga1", "gb1", "out0", "out1"])
BLOCK = {name: n for n, name in enumerate(BLOCKS)}
RING = 3

C_IDENT, C_UP, C_LOW, C_ONES, C_SLOW = (n * P for n in range(5))
C_NEG = 5 * P
C_SEL = 7 * P
C_F32 = 9 * P
R_QN, R_KN, R_ON, R_BR, R_DT, R_AL, R_FIRST = 0, 64, 128, 256, 292, 300, 308
R_ALL = 308 + EXP_PER_GROUP


def constants():
    i = np.arange(P)
    up = (i[:, None] <= i[None, :]).astype(np.float32)
    low = up.T.copy()
    slow = (i[:, None] < i[None, :]).astype(np.float32)
    neg = [(1 - up) * -BIG, (1 - low) * -BIG]
    sel = np.zeros((P, 2, P), np.float32)
    sel[0, 0], sel[1, 1] = 1, 1
    c = np.concatenate([np.eye(P, dtype=np.float32), up, low, np.ones((P, P), np.float32), slow, *neg,
                        sel.reshape(P, -1)], axis=1).astype(np.float32)
    lv = []
    for d in range(2):
        for n in LEVELS:
            b = i // n
            m = (b[None, :] % 2 == 1) & (b[:, None] == b[None, :] - 1)
            lv.append((m if d == 0 else m.T).astype(np.float32))
    return c, np.concatenate(lv, axis=1)


def build(nc, t):
    with ExitStack() as ctx:
        arena = ctx.enter_context(nc.sbuf_tensor("arena", [P, 53000], F32))
        banks = [ctx.enter_context(nc.psum_tensor(f"bank{n}", [P, HALF], F32)) for n in range(8)]
        sems = {}

        def sem(name):
            sems[name] = ctx.enter_context(nc.semaphore(name))
            return sems[name]

        top = [0]

        def cut(*shape):
            n = int(np.prod(shape))
            v = arena[:, top[0]:top[0] + n]
            top[0] += n
            assert top[0] <= 53000, top[0]
            if len(shape) == 2:
                v = v.rearrange("p (a b) -> p a b", a=shape[0])
            if len(shape) == 3:
                v = v.rearrange("p (a b c) -> p a b c", a=shape[0], b=shape[1])
            if len(shape) == 4:
                v = v.rearrange("p (a b c d) -> p a b c d", a=shape[0], b=shape[1], c=shape[2])
            return v

        const = cut(C_F32)
        ident, upper, lower = (const[:, o:o + P] for o in (C_IDENT, C_UP, C_LOW))
        ones, earlier = const[:, C_ONES:C_ONES + P], const[:, C_SLOW:C_SLOW + P]
        negmask = [const[:, C_NEG + d * P:C_NEG + (d + 1) * P] for d in range(2)]
        pick = [const[0:2, C_SEL + c * P:C_SEL + (c + 1) * P] for c in range(2)]
        rows = cut(R_ALL)
        cT = cut(KC * 2)
        silu_cT = cut(KC, 2)
        mod_row = cut(2, HALF)
        stat = cut(2, T)
        eps_col = cut(1)
        ring = cut(RING, KC * HALF)
        ringv = ring.rearrange("p s (k n) -> p s k n", k=KC)
        hT = cut(KC, TOK)
        oaT = cut(H_A // 2, TOK)
        shared = top[0]
        shift_bc = cut(2, D)
        scale_bc = cut(2, D)
        low_end = top[0]

        x_sb = cut(T, D)
        h_tok = cut(2, D)
        bmod_a = cut(4, HALF)
        norm_a = cut(D)
        norm_end = top[0]
        top[0] = low_end
        bias = cut(2, H_A, KEYS)
        vband = cut(2, 2, W_A)
        assert top[0] <= norm_end
        top[0] = norm_end
        qaT = cut(H_A // 2, TOK)
        qa_blocks = qaT[:, :, SEQ:TOK].rearrange("p a (m r c) -> p a m r c", m=N_CB, r=ROWS)
        kaT = cut(H_A // 2, TOK)
        va0 = cut(W_A)
        vctx = cut(W_A)
        kctx = cut(W_A)
        kctxT = cut(H_A // 2, PAST)
        square = cut(2, W_A)
        qk_tok = cut(2, W_A)
        va_out = cut(2, W_A)
        headstat = cut(2, 3 * H_A)
        score = cut(2, KEYS)
        probT = cut(2, KEYS)
        sstat = cut(2, 3)

        top[0] = low_end
        o_acc = cut(T, W_B)
        phase_c = top[0]
        level_mask = cut(2 * len(LEVELS) * P // 2).bitcast(BF16).rearrange("p (d n c) -> p d n c", d=2, n=len(LEVELS))
        rope = cut(4, 2, 64)
        conv_w = cut(12, CONV_K)
        w_ab = cut(KC, 16)
        ab = cut(T, 16)
        gt = cut(12, 2 * T * H_B)
        qkstat = cut(T, 16)
        qkv = cut(T, 3 * W_B)
        kdT = cut(H_B, TOK)
        qdT = cut(H_B, TOK)
        phase_b = top[0]
        xc = cut(2, XC)
        yc = cut(2, YC)
        ys = cut(2, YC)
        sq_b = cut(2, 2 * W_B)
        ropet = cut(4, 2 * H_B, 64)
        top[0] = phase_b
        unit = [{}, {}]
        for k in ("decayT", "gramT", "intraT", "mask0", "mask1", "xs", "inv", "invT"):
            unit[0][k] = cut(H_B, P)
            unit[1][k] = cut(H_B, P)
        top[0], back = shared, top[0]
        for k in ("erow", "kexp", "kend", "state"):
            unit[0][k] = cut(H_B, P)
            unit[1][k] = cut(H_B, P)
        top[0] = back
        for U in unit:
            U["nwT"] = U["mask0"]
            U["vnew"] = U["xs"]

        top[0] = phase_c
        gate1_bc = cut(2, D)
        gate2_bc = cut(2, D)
        osq = cut(2, W_B)
        ostat = cut(T, 8)
        zs = cut(2, W_B)
        obT = cut(H_B, TOK)
        sga = cut(2, HALF)
        sgb = cut(2, HALF)
        merged = cut(T, D)
        w_router = cut(KC, N_GROUPS + N_EXPERTS)
        combine = cut(T, N_EXPERTS)
        x2 = cut(T, D)
        logit = cut(T, N_GROUPS + N_EXPERTS)
        ex = cut(2, T, 5)
        gmax = cut(T, 1)
        gsel = cut(T, N_GROUPS)
        geq = cut(T, N_GROUPS)
        eprod = cut(T, N_GROUPS, EXP_PER_GROUP)
        ingrp = cut(T, EXP_PER_GROUP)
        eeq = cut(T, EXP_PER_GROUP)
        esel = cut(2, T, EXP_PER_GROUP)
        emax = cut(3, T, 1)
        wts = cut(3, T, 1)
        end = top[0]
        top[0] = phase_c + 2 * 2 * D + 2 * W_B + T * 8 + 2 * W_B
        h2_tok = cut(2, D)
        top[0] = phase_c + 2 * 2 * D + 4 * W_B + T * 8 + H_B * TOK + 4 * HALF
        bmod_c = cut(8, HALF)
        norm_c = cut(D)
        top[0] = end
        eup = [ringv[:, 0], ringv[:, 1]]
        edown = [ring[:, 2, n * 2 * D:(n + 1) * 2 * D].rearrange("p (k n) -> p k n", k=2) for n in range(2)]
        acc, sg, hid, hidT = merged, sga, zs, osq

        for n in ("consts_in", "kv_ctx_in", "b_in", "states_in", "c_in", "bias_in0", "bias_in1", "vband_in0", "vband_in1",
                  "silu_c", "mod_mm", "row_ready", "bc_mm", "bc_done", "rstd_ready", "ssq_ready", "h_ready",
                  "hT_mm", "hT_ready", "proj_mm", "proj_used", "squared", "headsum", "headstd", "qk_ready", "qkT_mm",
                  "qkT_ready", "va_ready", "kctxT_mm", "kctxT_ready", "k_out", "v_out",
                  "score_mm", "max_ready", "exp_done", "prob_ready", "probT_mm", "probT_ready", "pv_mm", "pv_used",
                  "ab_mm", "ab_used", "g_raw", "g_act", "g_ready", "gc_mm", "gc_used", "gexp_done",
                  "cm_mm", "xc_ready", "conv_ready", "ys_ready", "tok_mm", "tok_ready", "sq_ready", "qksum", "qkstd",
                  "rope_done", "kqT_mm", "kqT_ready", "phase", "pads",
                  "osq_ready", "osum", "ostd", "on_ready", "z_mm", "zs_ready", "ob_ready", "obT_mm", "obT_ready",
                  "merge_mm", "sig_ready", "merged_ready", "mT_mm", "mT_ready", "out_mm", "x2_ready",
                  "logit_mm", "logit_used", "router_exp_in", "router_exp", "combine_ready",
                  "eup_mm", "silu_done", "hid_ready", "hidT_mm", "hidT_ready", "down_mm", "acc_done", "y_ready",
                  "y_out", "state_out",
                  "dve_step", "act_step", "pool_step", "w_used", "e_used"):
            sem(n)
        for d in range(2):
            for n in ("row_mm", "kq_mm", "x_mm", "p_mm", "wt_mm", "vn_mm", "o_mm", "erow", "dexp", "xs", "nwt", "dpre",
                      "bt", "mn", "vn", "os", "prep", "msk", "st"):
                sem(f"{n}{d}")
        for s in range(RING):
            sem(f"w_in{s}")
        for s in range(2):
            sem(f"e_in{s}")
            sem(f"v_scratch{s}")
        for s in range(T):
            sem(f"x_in{s}")
        sem("mod_c_in")
        S = sems

        def w_slot(name):
            return BLOCK[name] % RING

        def w_wait(eng, name):
            eng.wait_ge(S[f"w_in{w_slot(name)}"], 16 * (BLOCK[name] // RING + 1))

        def read_by(name):
            kind, n = name[:-1], name[-1]
            if kind == "mod":
                return S["mod_mm"], int(name[3:]) + 1
            if name[:3] == "mod":
                return S["mod_mm"], int(name[3:]) + 1
            if name in ("qa", "ka", "va"):
                return S["proj_mm"], T * (("qa", "ka", "va").index(name) + 1)
            if name in ("qb", "kb", "vb"):
                return S["cm_mm"], 4 * (("qb", "kb", "vb").index(name) + 1)
            if name == "zb":
                return S["z_mm"], T
            if kind in ("proj", "ga", "gb"):
                return S["merge_mm"], T * (int(n) + 1)
            return S["out_mm"], T * (int(n) + 1)

        def stepper(eng, own):
            counts = {}

            def step(ins, signal=own):
                counts[signal] = counts.get(signal, 0) + 1
                ins.then_inc(S[signal], 1)
                eng.wait_ge(S[signal], counts[signal])

            return step

        def barrier(eng, n):
            eng.drain().then_inc(S["phase"], 1)
            eng.wait_ge(S["phase"], 4 * n)

        tok0 = [i * P for i in range(T)]
        block = ctx.enter_context(nc.Block())

        @block.sync
        def _(sp):
            sp.dma_start(cT, t["cT"]).then_inc(S["c_in"], 16)
            for n, name in enumerate(BLOCKS):
                if n >= RING:
                    sp.wait_ge(*read_by(BLOCKS[n - RING]))
                sp.dma_start(ring[:, n % RING, :], t["w_blocks"][n]).then_inc(S[f"w_in{n % RING}"], 16)
            for e in range(N_EXPERTS):
                if e == 0:
                    sp.wait_ge(*read_by("gb1"))
                    sp.wait_ge(*read_by("out1"))
                elif e >= 2:
                    sp.wait_ge(S["down_mm"], T * (e - 1))
                sp.dma_start(eup[e % 2], t["w_up"][e].rearrange("p (k n) -> p k n", k=KC)).then_inc(S[f"e_in{e % 2}"], 16)
                sp.dma_start(edown[e % 2], t["w_down"][e].rearrange("p (k n) -> p k n", k=2)).then_inc(S[f"e_in{e % 2}"], 16)
            for i in range(T):
                sp.wait_ge(S["y_ready"], i + 1)
                sp.dma_start(t["y"][i], x2[:, i, :]).then_inc(S["y_out"], 16)
            sp.wait_ge(S["y_out"], 16 * T)

        @block.gpsimd
        def _(pool):
            step = stepper(pool, "pool_step")
            pool.dma_start(const, t["const"]).then_inc(S["consts_in"], 16)
            pool.dma_start(rows, t["rows"]).then_inc(S["consts_in"], 16)
            pool.dma_start(bmod_a[0:2], t["bmod"][:, 0:4]).then_inc(S["consts_in"], 16)
            pool.dma_start(norm_a[0:2], t["norm_w"][:, 0]).then_inc(S["consts_in"], 16)
            for i in range(T):
                pool.dma_start(x_sb[:, i, :], t["x"][i]).then_inc(S[f"x_in{i}"], 16)
            pool.dma_start(kctx, t["kctx"]).then_inc(S["kv_ctx_in"], 16)
            pool.dma_start(vctx, t["vctx"]).then_inc(S["kv_ctx_in"], 16)
            pool.wait_ge(S["hT_ready"], 2 * T)
            for u in range(2):
                pool.dma_start(bias[:, u], t["bias"][u].rearrange("p (h k) -> p h k", h=H_A)).then_inc(S[f"bias_in{u}"], 16)
            pool.wait_ge(S["qk_ready"], T + 1)
            pool.dma_start(t["new_k"], qk_tok[:, T % 2, :]).then_inc(S["k_out"], 16)
            pool.wait_ge(S["va_ready"], 1)
            pool.dma_start(t["new_v"], va0).then_inc(S["v_out"], 16)
            for i in range(1, T):
                pool.wait_ge(S["va_ready"], i + 1)
                pool.dma_start(t["v_scratch"][i - 1], va_out[:, i % 2, :]).then_inc(S[f"v_scratch{i % 2}"], 16)
            for s in range(2):
                pool.wait_ge(S[f"v_scratch{s}"], 16 * (T - 1) // 2)
            grid = t["v_scratch"].rearrange("i (r c) d -> (i r) c d", c=GRID_W)
            for m in range(N_CB):
                if m >= 2:
                    pool.wait_ge(S["pv_mm"], 8 * m)
                for j in range(2):
                    for r in range(4):
                        pool.dma_start(vband[r * BAND_W:(r + 1) * BAND_W, m % 2, j, :],
                                       grid[4 * j + r, BAND_START[m]:BAND_START[m] + BAND_W, :]).then_inc(S[f"vband_in{m % 2}"], 16)
                if m == 3:
                    pool.dma_start(bias[:, 0], t["bias"][2].rearrange("p (h k) -> p h k", h=H_A)).then_inc(S["bias_in0"], 16)
            pool.wait_ge(S["k_out"], 16)
            pool.wait_ge(S["v_out"], 16)
            barrier(pool, 1)

            pool.dma_start(level_mask, t["level_mask"].rearrange("p (d n c) -> p d n c", d=2, n=len(LEVELS))).then_inc(S["b_in"], 16)
            pool.dma_start(rope, t["rope"].rearrange("p (a b c) -> p a b c", a=4, b=2)).then_inc(S["b_in"], 16)
            pool.dma_start(conv_w, t["conv_w"].rearrange("p (a b) -> p a b", a=12)).then_inc(S["b_in"], 16)
            pool.dma_start(w_ab, t["w_ab"].rearrange("p (a b) -> p a b", a=KC)).then_inc(S["b_in"], 16)
            pool.wait_ge(S["gexp_done"], 1)
            pool.wait_ge(S["kqT_ready"], 2 * T)
            pool.wait_ge(S["b_in"], 64)
            for p in range(T):
                for d in range(2):
                    U = unit[d]
                    i = 0 if p == 0 else (p if d == 0 else T - p)
                    if p == 1:
                        pool.wait_ge(S["state_out"], 32)
                        pool.dma_start(U["state"], t["state0"][d].rearrange("p (h c) -> p h c", h=H_B)).then_inc(S["states_in"], 16)
                    if p >= 1:
                        pool.wait_ge(S[f"o_mm{d}"], 2 * p)
                    col = (d * T + i) * H_B
                    step(pool.tensor_tensor(U["inv"], ident.unsqueeze(1).to_broadcast([P, H_B, P]),
                                            gt[:, 3, col:col + H_B].unsqueeze(2).to_broadcast([P, H_B, P]), ALU.mult))
                    step(pool.tensor_copy(U["invT"], U["inv"]), f"prep{d}")
                    k_i = qkv[:, i, W_B:2 * W_B].rearrange("p (h c) -> p h c", h=H_B)
                    step(pool.tensor_tensor(U["kexp"], k_i, gt[:, 4, col:col + H_B].unsqueeze(2).to_broadcast([P, H_B, P]), ALU.mult))
                    step(pool.tensor_tensor(U["kend"], k_i, gt[:, 5, col:col + H_B].unsqueeze(2).to_broadcast([P, H_B, P]), ALU.mult))
                    pool.wait_ge(S[f"erow{d}"], p + 1)
                    step(pool.tensor_tensor(U["erow"], U["erow"], qdT[:, :, tok0[i]:tok0[i] + P], ALU.mult), f"prep{d}")
                for n in range(len(LEVELS)):
                    for d in range(2):
                        U = unit[d]
                        if n == 0:
                            pool.wait_ge(S[f"bt{d}"], 2 * p + 1)
                        if n >= 2:
                            pool.wait_ge(S[f"x_mm{d}"], len(LEVELS) * p + n - 1)
                        step(pool.tensor_tensor(U[f"mask{n % 2}"], U["gramT"],
                                                level_mask[:, d, n, :].unsqueeze(1).to_broadcast([P, H_B, P]), ALU.mult), f"msk{d}")
                if p == 0:
                    for d in range(2):
                        pool.wait_ge(S[f"os{d}"], 2)
                        pool.dma_start(t["new_state"][d], unit[d]["state"]).then_inc(S["state_out"], 16)
            barrier(pool, 2)
            pool.dma_start(bmod_c[0:2], t["bmod"][:, 4:12]).then_inc(S["mod_c_in"], 16)
            pool.dma_start(norm_c[0:2], t["norm_w"][:, 1]).then_inc(S["mod_c_in"], 16)
            pool.dma_start(w_router, t["w_router"].rearrange("p (a b) -> p a b", a=KC)).then_inc(S["b_in"], 16)
            for i in range(T):
                pool.dma_start(x2[:, i, :], t["x"][i]).then_inc(S[f"x_in{i}"], 16)
            for i in range(T):
                pool.wait_ge(S[f"x_in{i}"], 32)
            barrier(pool, 3)

        @block.scalar
        def _(act):
            step = stepper(act, "act_step")
            sc = nc.scalar
            act.wait_ge(S["c_in"], 16)
            step(sc.activation(silu_cT, cT.rearrange("p (a b) -> p a b", a=KC), ACT.Silu), "silu_c")

            def bc_copy(j):
                dst = {0: shift_bc, 1: scale_bc, 2: gate1_bc, 3: shift_bc, 4: scale_bc, 5: gate2_bc}[j // 2]
                for c in range(2):
                    act.wait_ge(S["bc_mm"], 2 * j + c + 1)
                    step(sc.activation(dst[:, c, (j % 2) * HALF:(j % 2 + 1) * HALF], banks[2 + c][:, :], ACT.Copy), "bc_done")

            def norm_act(n, x):
                for i in range(T):
                    if n == 0:
                        act.wait_ge(S[f"x_in{i}"], 16)
                    else:
                        act.wait_ge(S["x2_ready"], T * NHALF)
                    step(sc.activation(hT[:, 0:2, 0:HALF], x[:, i, :].rearrange("p (a b) -> p a b", a=2), ACT.Square,
                                       accum_out=stat[:, 0, i:i + 1]))
                act.wait_ge(S["pads"], 1)
                step(sc.activation(stat[:, 0, :], stat[:, 0, :], ACT.Sqrt, bias=eps_col, scale=1.0 / D), "ssq_ready")

            def norm_out(n):
                for i in range(T):
                    for g in range(2):
                        act.wait_ge(S["hT_mm"], 2 * (n * T + i) + g + 1)
                        step(sc.activation(hT[:, 4 * g:4 * g + 4, tok0[i]:tok0[i] + P],
                                           banks[4 + g][:, :].rearrange("p (a b) -> p a b", a=4), ACT.Copy), "hT_ready")

            norm_act(0, x_sb)
            for j in range(4):
                bc_copy(j)
            norm_out(0)
            act.wait_ge(S["kctxT_mm"], 1)
            step(sc.activation(kctxT, banks[6][:, :].rearrange("p (a b) -> p a b", a=4), ACT.Copy), "kctxT_ready")
            for u in range(2 * T):
                act.wait_ge(S["proj_mm"], u + 1)
                if u >= 2:
                    act.wait_ge(S["headsum"], u - 1)
                step(sc.activation(square[:, u % 2, :], banks[u % 4][:, :], ACT.Square), "squared")
                act.wait_ge(S["headsum"], u + 1)
                step(sc.activation(headstat[:, u % 2, 8:16], headstat[:, u % 2, 0:8], ACT.Sqrt, bias=eps_col,
                                   scale=1.0 / D_HA), "headstd")
                if u >= 1:
                    v = u - 1
                    act.wait_ge(S["qkT_mm"], v + 1)
                    src = banks[4 + v % 2][:, :].rearrange("p (a b) -> p a b", a=4)
                    if 1 <= v < T:
                        for r in range(2):
                            step(sc.activation(qa_blocks[:, :, :, 2 * (v - 1) + r, :],
                                               src[:, :, r * GRID_W:(r + 1) * GRID_W].rearrange("p a (m c) -> p a m c", m=N_CB),
                                               ACT.Copy), "qkT_ready" if r else "act_step")
                    else:
                        step(sc.activation((qaT if v < T else kaT)[:, :, tok0[v % T]:tok0[v % T] + P], src, ACT.Copy), "qkT_ready")
            v = 2 * T - 1
            act.wait_ge(S["qkT_mm"], v + 1)
            step(sc.activation(kaT[:, :, tok0[T - 1]:tok0[T - 1] + P],
                               banks[4 + v % 2][:, :].rearrange("p (a b) -> p a b", a=4), ACT.Copy), "qkT_ready")
            for i in range(T):
                u = 2 * T + i
                act.wait_ge(S["proj_mm"], u + 1)
                if i >= 3:
                    act.wait_ge(S[f"v_scratch{i % 2}"], 16)
                dst = va0 if i == 0 else va_out[:, i % 2, :]
                step(sc.activation(dst, banks[u % 4][:, :], ACT.Copy), "va_ready")

            NU = 8 * (1 + N_CB)

            def probs_out(u):
                w = P if u < 8 else KEYS
                act.wait_ge(S["probT_mm"], u + 1)
                if u >= 2:
                    act.wait_ge(S["pv_mm"], u - 1)
                step(sc.activation(probT[:, u % 2, 0:w], banks[2 + u % 2][:, 0:w], ACT.Copy), "probT_ready")

            for u in range(NU):
                w = P if u < 8 else KEYS
                act.wait_ge(S["max_ready"], u + 1)
                step(sc.activation(score[:, u % 2, 0:w], score[:, u % 2, 0:w], ACT.Exp, bias=sstat[:, u % 2, 0:1],
                                   accum_out=sstat[:, u % 2, 1:2]), "exp_done")
                if u >= 1:
                    probs_out(u - 1)
            probs_out(NU - 1)
            barrier(act, 1)

            act.wait_ge(S["g_raw"], 1)
            step(sc.activation(gt[:, 6:8, :], gt[:, 1:3, :], ACT.Exp, scale=-1.0))
            step(sc.activation(gt[:, 8, 0:8], rows[:, R_AL:R_AL + 8], ACT.Exp))
            step(sc.activation(gt[:, 6, :], gt[:, 6, :], ACT.Ln, bias=ones[:, 0:1]), "g_act")
            act.wait_ge(S["gc_used"], 1)
            step(sc.activation(gt[:, 4:6, :], gt[:, 10:12, :], ACT.Exp))
            step(sc.activation(gt[:, 9, :], gt[:, 9, :], ACT.Exp), "gexp_done")

            def silu_out(c):
                act.wait_ge(S["conv_ready"], c + 1)
                if c >= 2:
                    act.wait_ge(S["tok_mm"], c - 1)
                step(sc.activation(ys[:, c % 2, :], yc[:, c % 2, :], ACT.Silu), "ys_ready")

            for c in range(12):
                act.wait_ge(S["cm_mm"], c + 1)
                if c >= 2:
                    act.wait_ge(S["conv_ready"], c - 1)
                else:
                    act.wait_ge(S["pads"], 2)
                step(sc.activation(xc[:, c % 2, 2:2 + SEQ], banks[2 * (c % 2) + 1][:, 0:SEQ], ACT.Copy))
                step(sc.activation(xc[:, c % 2, 4 + SEQ:4 + TOK], banks[2 * (c % 2)][:, :], ACT.Copy), "xc_ready")
                if c >= 1:
                    silu_out(c - 1)
            silu_out(11)
            for i in range(T):
                if i == 0:
                    act.wait_ge(S["tok_ready"], 12)
                if i >= 2:
                    act.wait_ge(S["qksum"], i - 1)
                step(sc.activation(sq_b[:, i % 2, :], qkv[:, i, 0:2 * W_B], ACT.Square), "sq_ready")
            act.wait_ge(S["qksum"], T)
            step(sc.activation(qkstat[:, :, 8:16], qkstat[:, :, 0:8], ACT.Sqrt, bias=eps_col), "qkstd")
            for i in range(T):
                for g in range(2):
                    act.wait_ge(S["kqT_mm"], 2 * i + g + 1)
                    step(sc.activation((qdT, kdT)[g][:, :, tok0[i]:tok0[i] + P],
                                       banks[2 * (i % 2) + g][:, :].rearrange("p (a b) -> p a b", a=4), ACT.Copy), "kqT_ready")
            
            for p in range(T):
                for d in range(2):
                    U = unit[d]
                    B0 = banks[4 * d][:, :].rearrange("p (h c) -> p h c", h=H_B)
                    act.wait_ge(S[f"row_mm{d}"], p + 1)
                    if p >= 1:
                        act.wait_ge(S[f"o_mm{d}"], 2 * p)
                    step(sc.activation(U["erow"], B0, ACT.Exp), f"erow{d}")
                    act.wait_ge(S[f"dpre{d}"], p + 1)
                    step(sc.activation(U["decayT"], U["decayT"], ACT.Exp), f"dexp{d}")
                for n in range(len(LEVELS)):
                    for d in range(2):
                        U = unit[d]
                        B0 = banks[4 * d][:, :].rearrange("p (h c) -> p h c", h=H_B)
                        act.wait_ge(S[f"x_mm{d}"], len(LEVELS) * p + n + 1)
                        if n >= 1:
                            act.wait_ge(S[f"p_mm{d}"], len(LEVELS) * p + n)
                        step(sc.activation(U["xs"], B0, ACT.Copy), f"xs{d}")
                for d in range(2):
                    U = unit[d]
                    B0 = banks[4 * d][:, :].rearrange("p (h c) -> p h c", h=H_B)
                    act.wait_ge(S[f"wt_mm{d}"], p + 1)
                    step(sc.activation(U["nwT"], B0, ACT.Copy, scale=-1.0), f"nwt{d}")
            barrier(act, 2)

            for i in range(T):
                if i >= 2:
                    act.wait_ge(S["osum"], i - 1)
                step(sc.activation(osq[:, i % 2, :], o_acc[:, i, :], ACT.Square), "osq_ready")
            act.wait_ge(S["osum"], T)
            step(sc.activation(ostat[:, :, 4:8], ostat[:, :, 0:4], ACT.Sqrt, bias=eps_col, scale=1.0 / DK), "ostd")

            def ob_out(i):
                act.wait_ge(S["obT_mm"], i + 1)
                step(sc.activation(obT[:, :, tok0[i]:tok0[i] + P],
                                   banks[4 + i % 2][:, :].rearrange("p (a b) -> p a b", a=4), ACT.Copy), "obT_ready")

            for i in range(T):
                act.wait_ge(S["z_mm"], i + 1)
                if i >= 2:
                    act.wait_ge(S["ob_ready"], i - 1)
                step(sc.activation(zs[:, i % 2, :], banks[i % 2][:, :], ACT.Silu), "zs_ready")
                if i >= 1:
                    ob_out(i - 1)
            ob_out(T - 1)
            for j in range(4, 12):
                bc_copy(j)
            for u in range(NHALF * T):
                b = 4 * (u % 2)
                act.wait_ge(S["merge_mm"], u + 1)
                if u >= 2:
                    act.wait_ge(S["merged_ready"], u - 1)
                step(sc.activation(sga[:, u % 2, :], banks[b + 2][:, :], ACT.Sigmoid))
                step(sc.activation(sgb[:, u % 2, :], banks[b + 3][:, :], ACT.Sigmoid), "sig_ready")
            for i in range(T):
                for g in range(2):
                    act.wait_ge(S["mT_mm"], 2 * i + g + 1)
                    step(sc.activation(hT[:, 4 * g:4 * g + 4, tok0[i]:tok0[i] + P],
                                       banks[4 + g][:, :].rearrange("p (a b) -> p a b", a=4), ACT.Copy), "mT_ready")
            act.wait_ge(S["out_mm"], T * NHALF)
            norm_act(1, x2)
            norm_out(1)
            act.wait_ge(S["router_exp_in"], 1)
            step(sc.activation(ex[:, 1], ex[:, 0], ACT.Exp), "router_exp")
            barrier(act, 3)

            def hid_out(u):
                act.wait_ge(S["hidT_mm"], u + 1)
                if u >= 2:
                    act.wait_ge(S["down_mm"], u - 1)
                step(sc.activation(hidT[:, u % 2, 0:2 * P], banks[2 + u % 2][:, 0:2 * P], ACT.Copy), "hidT_ready")

            for u in range(N_EXPERTS * T):
                act.wait_ge(S["eup_mm"], u + 1)
                if u >= 2:
                    act.wait_ge(S["hid_ready"], u - 1)
                step(sc.activation(sg[:, u % 2, 0:D_FF], banks[u % 2][:, 0:D_FF], ACT.Silu), "silu_done")
                if u >= 1:
                    hid_out(u - 1)
            hid_out(N_EXPERTS * T - 1)

        @block.vector
        def _(dve):
            step = stepper(dve, "dve_step")
            v = nc.vector
            step(v.memset(eps_col, EPS), "pads")
            dve.wait_ge(S["consts_in"], 64)

            def mod_rows(j):
                dve.wait_ge(S["mod_mm"], j + 1)
                if j >= 2:
                    dve.wait_ge(S["bc_mm"], 2 * (j - 1))
                r = mod_row[0:2, j % 2, :]
                kind, half = j // 2, j % 2
                b = bmod_a[0:2, j, :] if j < 4 else bmod_c[0:2, j - 4, :]
                if kind in (1, 4):
                    step(v.tensor_tensor(r, banks[j % 2][0:2, :], b, ALU.add))
                    step(v.scalar_tensor_tensor(r, r, 1.0, (norm_a, norm_c)[kind // 3][0:2, half * HALF:(half + 1) * HALF],
                                                ALU.add, ALU.mult), "row_ready")
                else:
                    step(v.tensor_tensor(r, banks[j % 2][0:2, :], b, ALU.add), "row_ready")

            def norm_dve(n, x, h):
                dve.wait_ge(S["ssq_ready"], n + 1)
                step(v.reciprocal(stat[:, 1, :], stat[:, 0, :]), "rstd_ready")
                dve.wait_ge(S["bc_done"], (8, 24)[n])
                for i in range(T):
                    c = min(i, 1)
                    if i >= 2:
                        dve.wait_ge(S["hT_mm"], 2 * (n * T + i - 1))
                    step(v.scalar_tensor_tensor(h[:, i % 2, :], x[:, i, :], stat[:, 1, i:i + 1], scale_bc[:, c, :], ALU.mult, ALU.mult))
                    step(v.tensor_tensor(h[:, i % 2, :], h[:, i % 2, :], shift_bc[:, c, :], ALU.add), "h_ready")

            for j in range(4):
                mod_rows(j)
            norm_dve(0, x_sb, h_tok)
            dve.wait_ge(S["hT_mm"], 2 * T)
            for u in range(2 * T):
                hs = headstat[:, u % 2, :]
                dve.wait_ge(S["squared"], u + 1)
                step(v.tensor_reduce(hs[:, 0:8], square[:, u % 2, :].rearrange("p (h c) -> p h c", h=H_A), AX_X, ALU.add), "headsum")
                dve.wait_ge(S["headstd"], u + 1)
                step(v.reciprocal(hs[:, 16:24], hs[:, 8:16]))
                if u >= 2:
                    dve.wait_ge(S["qkT_mm"], u - 1)
                if u == T + 2:
                    dve.wait_ge(S["k_out"], 16)
                q = qk_tok[:, u % 2, :].rearrange("p (h c) -> p h c", h=H_A)
                step(v.tensor_tensor(q, banks[u % 4][:, :].rearrange("p (h c) -> p h c", h=H_A),
                                     hs[:, 16:24].unsqueeze(2).to_broadcast([P, H_A, D_HA]), ALU.mult))
                w = rows[:, R_QN:R_QN + 64] if u < T else rows[:, R_KN:R_KN + 64]
                step(v.tensor_tensor(q, q, w.unsqueeze(1).to_broadcast([P, H_A, D_HA]), ALU.mult), "qk_ready")

            NU = 8 * (1 + N_CB)

            def pv_out(u):
                pair = u // 2
                dve.wait_ge(S["pv_mm"], 2 * pair + 2)
                b = banks[4 + pair % 2]
                h2 = pair % 4
                if u < 8:
                    dst, src = oaT[:, h2, 0:SEQ], b[:, 0:P]
                else:
                    m = u // 8 - 1
                    dst = oaT[:, h2, SEQ:TOK].rearrange("p (r c) -> p r c", c=GRID_W)[:, :, m * QB_W:(m + 1) * QB_W]
                    src = b[:, 0:P].rearrange("p (r c) -> p r c", c=QB_W)
                step(v.tensor_copy(dst, src), "pv_used")

            for u in range(NU):
                w = P if u < 8 else KEYS
                s = score[:, u % 2, 0:w]
                dve.wait_ge(S["score_mm"], u + 1)
                if u >= 2:
                    dve.wait_ge(S["probT_mm"], u - 1)
                if u < 8:
                    step(v.tensor_scalar(s, banks[u % 2][:, 0:w], D_HA ** -0.5, None, ALU.mult))
                else:
                    m, h = u // 8 - 1, u % 8
                    if h == 0:
                        dve.wait_ge(S[f"bias_in{BIAS_OF[m] % 2}"], 16 * (BIAS_OF[m] // 2 + 1))
                    step(v.scalar_tensor_tensor(s, banks[u % 2][:, 0:w], D_HA ** -0.5, bias[:, BIAS_OF[m] % 2, h, :], ALU.mult, ALU.add))
                step(v.tensor_reduce(sstat[:, u % 2, 0:1], s, AX_X, ALU.max, negate=True), "max_ready")
                dve.wait_ge(S["exp_done"], u + 1)
                step(v.reciprocal(sstat[:, u % 2, 2:3], sstat[:, u % 2, 1:2]))
                step(v.tensor_scalar(s, s, sstat[:, u % 2, 2:3], None, ALU.mult), "prob_ready")
                if u >= 3 and u % 2 == 1:
                    pv_out(u - 2)
            pv_out(NU - 1)
            barrier(dve, 1)

            step(v.memset(xc, 0.0), "pads")
            dve.wait_ge(S["b_in"], 64)
            dve.wait_ge(S["ab_mm"], 1)
            step(v.tensor_copy(ab, banks[7][:, 0:T * 16].rearrange("p (a b) -> p a b", a=T)), "ab_used")
            a_by_dir = ab[:, :, 0:8].rearrange("p t (d h) -> p d t h", d=2)
            b_by_dir = ab[:, :, 8:16].rearrange("p t (d h) -> p d t h", d=2)
            for d in range(2):
                g0 = gt[:, 0, d * T * H_B:(d + 1) * T * H_B].rearrange("p (t h) -> p t h", t=T)
                step(v.tensor_tensor(g0, a_by_dir[:, d], rows[:, R_DT + 4 * d:R_DT + 4 * d + 4].unsqueeze(1).to_broadcast([P, T, H_B]), ALU.add))
                step(v.tensor_copy(gt[:, 2, d * T * H_B:(d + 1) * T * H_B].rearrange("p (t h) -> p t h", t=T), b_by_dir[:, d]))
            step(v.scalar_tensor_tensor(gt[:, 1, :], gt[:, 0, :], -1.0, gt[:, 0, :], ALU.mult, ALU.max), "g_raw")
            dve.wait_ge(S["g_act"], 1)
            step(v.scalar_tensor_tensor(gt[:, 6, :], gt[:, 0, :], 0.0, gt[:, 6, :], ALU.max, ALU.add))
            for d in range(2):
                gd = gt[:, 0, d * T * H_B:(d + 1) * T * H_B].rearrange("p (t h) -> p t h", t=T)
                sd = gt[:, 6, d * T * H_B:(d + 1) * T * H_B].rearrange("p (t h) -> p t h", t=T)
                step(v.scalar_tensor_tensor(gd, sd, -1.0, gt[:, 8, 4 * d:4 * d + 4].unsqueeze(1).to_broadcast([P, T, H_B]), ALU.mult, ALU.mult))
            step(v.tensor_scalar(gt[:, 7, :], gt[:, 7, :], 1.0, None, ALU.add))
            step(v.reciprocal(gt[:, 3, :], gt[:, 7, :]), "g_ready")
            dve.wait_ge(S["gc_mm"], 1)
            n = 2 * T * H_B
            step(v.tensor_copy(gt[:, 9:11, :], banks[7][:, 128:128 + 2 * n].rearrange("p (a b) -> p a b", a=2)))
            step(v.tensor_tensor(gt[:, 11, :], gt[:, 9, :], gt[:, 10, :], ALU.subtract), "gc_used")

            def tok_out(c):
                dve.wait_ge(S["tok_mm"], c + 1)
                b = 4 + 2 * (c % 2)
                step(v.tensor_copy(qkv[:, 0, c * P:(c + 1) * P], banks[b + 1][:, 0:P]))
                step(v.tensor_copy(qkv[:, 1:T, c * P:(c + 1) * P], banks[b][:, :].rearrange("p (a b) -> p a b", a=4)), "tok_ready")

            for c in range(12):
                dve.wait_ge(S["xc_ready"], c + 1)
                if c >= 2:
                    dve.wait_ge(S["ys_ready"], c - 1)
                y = yc[:, c % 2, :]
                step(v.tensor_scalar(y, xc[:, c % 2, 0:YC], conv_w[:, c, 0:1], None, ALU.mult))
                for j in range(1, CONV_K):
                    step(v.scalar_tensor_tensor(y, xc[:, c % 2, j:j + YC], conv_w[:, c, j:j + 1], y, ALU.mult, ALU.add),
                         "conv_ready" if j == CONV_K - 1 else "dve_step")
                if c >= 1:
                    tok_out(c - 1)
            tok_out(11)
            for i in range(T):
                dve.wait_ge(S["sq_ready"], i + 1)
                step(v.tensor_reduce(qkstat[:, i, 0:8], sq_b[:, i % 2, :].rearrange("p (h c) -> p h c", h=8), AX_X, ALU.add), "qksum")
            dve.wait_ge(S["qkstd"], 1)
            step(v.reciprocal(qkstat[:, :, 0:8], qkstat[:, :, 8:16]))
            step(v.tensor_scalar(qkstat[:, :, 0:4], qkstat[:, :, 0:4], DK ** -0.5, None, ALU.mult))
            for i in range(T):
                qk = qkv[:, i, 0:2 * W_B].rearrange("p (h c) -> p h c", h=8)
                step(v.tensor_tensor(qk, qk, qkstat[:, i, 0:8].unsqueeze(2).to_broadcast([P, 8, DK]), ALU.mult),
                     "rope_done" if i == 0 else "dve_step")
                if i >= 1:
                    pairs = qkv[:, i, 0:2 * W_B].rearrange("p (h c two) -> p h c two", h=8, two=2)
                    x1, x2_ = pairs[:, :, :, 0], pairs[:, :, :, 1]
                    cos = rope[:, i - 1, 0, :].unsqueeze(1).to_broadcast([P, 8, 64])
                    sin = rope[:, i - 1, 1, :].unsqueeze(1).to_broadcast([P, 8, 64])
                    step(v.tensor_tensor(ropet[:, 0], x1, cos, ALU.mult))
                    step(v.tensor_tensor(ropet[:, 1], x2_, sin, ALU.mult))
                    step(v.tensor_tensor(ropet[:, 2], x1, sin, ALU.mult))
                    step(v.tensor_tensor(ropet[:, 3], x2_, cos, ALU.mult))
                    step(v.tensor_tensor(x1, ropet[:, 0], ropet[:, 1], ALU.subtract))
                    step(v.tensor_tensor(x2_, ropet[:, 2], ropet[:, 3], ALU.add), "rope_done")
            dve.wait_ge(S["kqT_ready"], 2 * T)
            dve.wait_ge(S["gexp_done"], 1)
            for d in range(2):
                step(v.memset(unit[d]["state"], 0.0), f"st{d}")
            for p in range(T):
                for d in range(2):
                    U = unit[d]
                    i = 0 if p == 0 else (p if d == 0 else T - p)
                    col = (d * T + i) * H_B
                    A = banks[4 * d][:, :].rearrange("p (h c) -> p h c", h=H_B)
                    B = banks[4 * d + 1][:, :].rearrange("p (h c) -> p h c", h=H_B)
                    C = banks[4 * d + 2][:, :].rearrange("p (h c) -> p h c", h=H_B)
                    dve.wait_ge(S[f"row_mm{d}"], p + 1)
                    dve.wait_ge(S[f"erow{d}"], p + 1)
                    for h in range(H_B):
                        step(v.scalar_tensor_tensor(U["decayT"][:, h], A[:, h], gt[:, 10, col + h:col + h + 1], negmask[d],
                                                    ALU.subtract, ALU.add), f"dpre{d}" if h == H_B - 1 else "dve_step")
                    dve.wait_ge(S[f"dexp{d}"], p + 1)
                    dve.wait_ge(S[f"kq_mm{d}"], p + 1)
                    if p >= 1:
                        dve.wait_ge(S[f"o_mm{d}"], 2 * p)
                    step(v.tensor_tensor(U["gramT"], B, U["decayT"], ALU.mult), f"bt{d}")
                    step(v.tensor_tensor(U["intraT"], C, U["decayT"], ALU.mult), f"bt{d}")
                for n in range(len(LEVELS)):
                    for d in range(2):
                        U = unit[d]
                        B = banks[4 * d + 1][:, :].rearrange("p (h c) -> p h c", h=H_B)
                        C = banks[4 * d + 2][:, :].rearrange("p (h c) -> p h c", h=H_B)
                        dve.wait_ge(S[f"p_mm{d}"], len(LEVELS) * p + n + 1)
                        step(v.tensor_tensor(U["inv"], U["inv"], B, ALU.subtract))
                        step(v.tensor_tensor(U["invT"], U["invT"], C, ALU.subtract), f"mn{d}")
                for d in range(2):
                    U = unit[d]
                    B = banks[4 * d + 1][:, :].rearrange("p (h c) -> p h c", h=H_B)
                    dve.wait_ge(S[f"vn_mm{d}"], p + 1)
                    step(v.tensor_copy(U["vnew"], B), f"vn{d}")
                for d in range(2):
                    U = unit[d]
                    i = 0 if p == 0 else (p if d == 0 else T - p)
                    col = (d * T + i) * H_B
                    C = banks[4 * d + 2][:, :].rearrange("p (h c) -> p h c", h=H_B)
                    O = banks[4 * d + 3][:, :]
                    first = d == 0 if p == 0 else p <= 2
                    dve.wait_ge(S[f"o_mm{d}"], 2 * p + 1)
                    if first:
                        step(v.tensor_copy(o_acc[:, i, :], O), f"os{d}")
                    else:
                        step(v.tensor_tensor(o_acc[:, i, :], o_acc[:, i, :], O, ALU.add), f"os{d}")
                    dve.wait_ge(S[f"o_mm{d}"], 2 * p + 2)
                    for h in range(H_B):
                        step(v.scalar_tensor_tensor(U["state"][:, h], U["state"][:, h], gt[:, 9, col + h:col + h + 1], C[:, h],
                                                    ALU.mult, ALU.add), f"os{d}" if h == H_B - 1 else "dve_step")
                if p == 0:
                    dve.wait_ge(S["states_in"], 32)
            barrier(dve, 2)

            for i in range(T):
                dve.wait_ge(S["osq_ready"], i + 1)
                step(v.tensor_reduce(ostat[:, i, 0:4], osq[:, i % 2, :].rearrange("p (h c) -> p h c", h=4), AX_X, ALU.add), "osum")
            dve.wait_ge(S["ostd"], 1)
            step(v.reciprocal(ostat[:, :, 0:4], ostat[:, :, 4:8]))
            onw = rows[:, R_ON:R_ON + DK].unsqueeze(1).to_broadcast([P, H_B, DK])
            for i in range(T):
                o = o_acc[:, i, :].rearrange("p (h c) -> p h c", h=4)
                step(v.tensor_tensor(o, o,
                                     ostat[:, i, 0:4].unsqueeze(2).to_broadcast([P, H_B, DK]), ALU.mult))
                step(v.tensor_tensor(o, o, onw, ALU.mult))
                dve.wait_ge(S["zs_ready"], i + 1)
                step(v.tensor_tensor(o_acc[:, i, :], o_acc[:, i, :], zs[:, i % 2, :], ALU.mult), "ob_ready")
            dve.wait_ge(S["mod_c_in"], 32)
            for j in range(4, 12):
                mod_rows(j)
            for u in range(NHALF * T):
                n, i = u // T, u % T
                b = 4 * (u % 2)
                dve.wait_ge(S["sig_ready"], u + 1)
                step(v.tensor_tensor(sga[:, u % 2, :], sga[:, u % 2, :], banks[b][:, :], ALU.mult))
                step(v.tensor_tensor(sgb[:, u % 2, :], sgb[:, u % 2, :], banks[b + 1][:, :], ALU.mult))
                step(v.tensor_tensor(merged[:, i, n * HALF:(n + 1) * HALF], sga[:, u % 2, :], sgb[:, u % 2, :], ALU.add), "merged_ready")
            for i in range(T):
                dve.wait_ge(S[f"x_in{i}"], 32)
            for u in range(NHALF * T):
                n, i = u // T, u % T
                c = min(i, 1)
                cols = slice(n * HALF, (n + 1) * HALF)
                dve.wait_ge(S["out_mm"], u + 1)
                step(v.tensor_tensor(sga[:, u % 2, :], gate1_bc[:, c, cols], banks[u % 4][:, :], ALU.mult))
                step(v.tensor_tensor(x2[:, i, cols], x2[:, i, cols], sga[:, u % 2, :], ALU.add), "x2_ready")
            norm_dve(1, x2, h2_tok)
            first4 = rows[:, R_FIRST + 4:R_FIRST + 8].unsqueeze(1).to_broadcast([P, T, 4])
            first8 = rows[:, R_FIRST:R_FIRST + 8].unsqueeze(1).to_broadcast([P, T, 8])
            dve.wait_ge(S["logit_mm"], 1)
            step(v.tensor_tensor(logit, banks[0][:, 0:T * 36].rearrange("p (t n) -> p t n", t=T),
                                 rows[:, R_BR:R_BR + 36].unsqueeze(1).to_broadcast([P, T, 36]), ALU.add))
            groups = logit[:, :, 0:N_GROUPS]
            step(v.tensor_reduce(gmax, groups, AX_X, ALU.max))
            step(v.tensor_tensor(ex[:, 0, :, 0:4], groups, gmax.to_broadcast([P, T, 4]), ALU.subtract))
            step(v.tensor_tensor(geq, groups, gmax.to_broadcast([P, T, 4]), ALU.is_equal))
            step(v.tensor_tensor(geq, geq, first4, ALU.mult))
            step(v.tensor_reduce(gmax, geq, AX_X, ALU.max))
            step(v.tensor_tensor(gsel, geq, gmax.to_broadcast([P, T, 4]), ALU.is_equal))
            step(v.tensor_tensor(eprod, logit[:, :, N_GROUPS:].rearrange("p t (g e) -> p t g e", g=N_GROUPS),
                                 gsel.unsqueeze(3).to_broadcast([P, T, 4, 8]), ALU.mult))
            step(v.tensor_reduce(ingrp, eprod.rearrange("p t g e -> p t e g"), AX_X, ALU.add))
            for r in range(2):
                step(v.tensor_reduce(emax[:, r], ingrp, AX_X, ALU.max))
                step(v.tensor_tensor(eeq, ingrp, emax[:, r].to_broadcast([P, T, 8]), ALU.is_equal))
                step(v.tensor_tensor(eeq, eeq, first8, ALU.mult))
                step(v.tensor_reduce(emax[:, 2], eeq, AX_X, ALU.max))
                step(v.tensor_tensor(esel[:, r], eeq, emax[:, 2].to_broadcast([P, T, 8]), ALU.is_equal))
                if r == 0:
                    step(v.scalar_tensor_tensor(ingrp, esel[:, 0], -BIG, ingrp, ALU.mult, ALU.add))
            step(v.tensor_tensor(ex[:, 0, :, 4:5], emax[:, 1], emax[:, 0], ALU.subtract), "router_exp_in")
            dve.wait_ge(S["router_exp"], 1)
            step(v.tensor_reduce(wts[:, 0], ex[:, 1, :, 0:4], AX_X, ALU.add))
            step(v.scalar_tensor_tensor(wts[:, 0], ex[:, 1, :, 4:5], 1.0, wts[:, 0], ALU.add, ALU.mult))
            step(v.reciprocal(wts[:, 1], wts[:, 0]))
            step(v.tensor_tensor(wts[:, 2], wts[:, 1], ex[:, 1, :, 4:5], ALU.mult))
            for r in range(2):
                step(v.tensor_tensor(esel[:, r], esel[:, r], wts[:, 1 + r].to_broadcast([P, T, 8]), ALU.mult))
            step(v.tensor_tensor(eeq, esel[:, 0], esel[:, 1], ALU.add))
            step(v.tensor_tensor(combine.rearrange("p t (g e) -> p t g e", g=N_GROUPS), eeq.unsqueeze(2).to_broadcast([P, T, 4, 8]),
                                 gsel.unsqueeze(3).to_broadcast([P, T, 4, 8]), ALU.mult), "combine_ready")
            barrier(dve, 3)

            step(v.memset(acc, 0.0))

            def acc_add(u):
                dve.wait_ge(S["down_mm"], u + 1)
                for n in range(NHALF):
                    part = acc[:, u % T, n * HALF:(n + 1) * HALF]
                    step(v.tensor_tensor(part, part, banks[4 + 2 * (u % 2) + n][:, :], ALU.add), "acc_done" if n else "dve_step")

            for u in range(N_EXPERTS * T):
                e, i = u // T, u % T
                dve.wait_ge(S["silu_done"], u + 1)
                if u >= 2:
                    dve.wait_ge(S["hidT_mm"], u - 1)
                step(v.scalar_tensor_tensor(hid[:, u % 2, 0:D_FF], sg[:, u % 2, 0:D_FF], combine[:, i, e:e + 1],
                                            banks[u % 2][:, D_FF:2 * D_FF], ALU.mult, ALU.mult), "hid_ready")
                if u >= 1:
                    acc_add(u - 1)
            acc_add(N_EXPERTS * T - 1)
            for i in range(T):
                c = min(i, 1)
                step(v.tensor_tensor(acc[:, i, :], acc[:, i, :], gate2_bc[:, c, :], ALU.mult))
                step(v.tensor_tensor(x2[:, i, :], x2[:, i, :], acc[:, i, :], ALU.add), "y_ready")

        @block.tensor
        def _(pe):
            mm = nc.tensor.matmul

            def mod_mm(j):
                w = ringv[:, w_slot(f"mod{j}")]
                if j == 0:
                    pe.wait_ge(S["silu_c"], 1)
                w_wait(pe, f"mod{j}")
                if j >= 2:
                    pe.wait_ge(S["row_ready"], j - 1)
                for k in range(KC):
                    last = mm(banks[j % 2][0:2, :], silu_cT[:, k, :], w[:, k, :], start=(k == 0), stop=(k == KC - 1))
                last.then_inc(S["mod_mm"], 1)

            def mod_bc(j):
                pe.wait_ge(S["row_ready"], j + 1)
                pe.wait_ge(S["consts_in"], 64)
                for c in range(2):
                    if j >= 1:
                        pe.wait_ge(S["bc_done"], 2 * (j - 1) + c + 1)
                    last = mm(banks[2 + c][:, :], pick[c], mod_row[0:2, j % 2, :], start=True, stop=True)
                    last.then_inc(S["bc_mm"], 1)

            def turns(n, h):
                for i in range(T):
                    pe.wait_ge(S["h_ready"], n * T + i + 1)
                    for g in range(2):
                        if n * T + i >= 1:
                            pe.wait_ge(S["hT_ready"], 2 * (n * T + i) - 1 + g)
                        for a in range(4):
                            k = 4 * g + a
                            last = nc.tensor.transpose(banks[4 + g][:, a * P:(a + 1) * P], h[:, i % 2, k * P:(k + 1) * P], ident)
                        last.then_inc(S["hT_mm"], 1)

            def rows_mm(bank, name, i, cols=HALF):
                w = ringv[:, w_slot(name)]
                for k in range(KC):
                    last = mm(bank, hT[:, k, tok0[i]:tok0[i] + P], w[:, k, :], start=(k == 0), stop=(k == KC - 1))
                return last

            for j in range(4):
                mod_mm(j)
                if j >= 1:
                    mod_bc(j - 1)
            mod_bc(3)
            turns(0, h_tok)
            pe.wait_ge(S["kv_ctx_in"], 32)
            for a in range(4):
                last = nc.tensor.transpose(banks[6][:, a * P:(a + 1) * P], kctx[:, a * P:(a + 1) * P], ident)
            last.then_inc(S["kctxT_mm"], 1)

            def qk_turn(v):
                pe.wait_ge(S["qk_ready"], v + 1)
                if v >= 2:
                    pe.wait_ge(S["qkT_ready"], v - 1)
                else:
                    pe.wait_ge(S["hT_ready"], 2 * T)
                for a in range(4):
                    last = nc.tensor.transpose(banks[4 + v % 2][:, a * P:(a + 1) * P], qk_tok[:, v % 2, a * P:(a + 1) * P], ident)
                last.then_inc(S["qkT_mm"], 1)

            pe.wait_ge(S["hT_ready"], 2 * T)
            for u in range(3 * T):
                name = ("qa", "ka", "va")[u // T]
                if u % T == 0:
                    w_wait(pe, name)
                if u >= 4:
                    if u - 4 < 2 * T:
                        pe.wait_ge(S["qk_ready"], u - 3)
                    else:
                        pe.wait_ge(S["va_ready"], u - 3 - 2 * T)
                elif u < 4:
                    pe.wait_ge(S["bc_done"], 8)
                rows_mm(banks[u % 4][:, :], name, u % T).then_inc(S["proj_mm"], 1)
                if 1 <= u <= 2 * T:
                    qk_turn(u - 1)

            NU = 8 * (1 + N_CB)

            def scores(u):
                h = u % 8
                lanes = slice(64 * (h % 2), 64 * (h % 2) + 64)
                if u >= 2:
                    pe.wait_ge(S["max_ready"], u - 1)
                else:
                    pe.wait_ge(S["va_ready"], T)
                    pe.wait_ge(S["qkT_ready"], 2 * T)
                    pe.wait_ge(S["kctxT_ready"], 1)
                bank = banks[u % 2]
                if u < 8:
                    last = mm(bank[:, 0:SEQ], qaT[lanes, h // 2, 0:SEQ], kaT[lanes, h // 2, 0:SEQ], start=True, stop=True)
                else:
                    m = u // 8 - 1
                    q = qaT[lanes, h // 2, SEQ + m * P:SEQ + (m + 1) * P]
                    k = kaT[lanes, h // 2, SEQ:TOK].rearrange("p (r c) -> p r c", c=GRID_W)[:, :, BAND_START[m]:BAND_START[m] + BAND_W]
                    mm(bank[:, 0:BAND].rearrange("p (r c) -> p r c", c=BAND_W), q, k, start=True, stop=True)
                    last = mm(bank[:, BAND:KEYS], q, kctxT[lanes, h // 2, :], start=True, stop=True)
                last.then_inc(S["score_mm"], 1)

            def prob_turn(u):
                n = 1 if u < 8 else 3
                pe.wait_ge(S["prob_ready"], u + 1)
                if u >= 2:
                    pe.wait_ge(S["probT_ready"], u - 1)
                for a in range(n):
                    last = nc.tensor.transpose(banks[2 + u % 2][:, a * P:(a + 1) * P], score[:, u % 2, a * P:(a + 1) * P], ident)
                last.then_inc(S["probT_mm"], 1)

            def values(u):
                h = u % 8
                pair = u // 2
                out = banks[4 + pair % 2][64 * (u % 2):64 * (u % 2) + 64, 0:P]
                pe.wait_ge(S["probT_ready"], u + 1)
                if pair >= 2 and u % 2 == 0:
                    pe.wait_ge(S["pv_used"], pair - 1)
                hc = slice(h * D_HA, (h + 1) * D_HA)
                if u < 8:
                    last = mm(out, va0[:, hc], probT[:, u % 2, 0:P], start=True, stop=True)
                else:
                    m = u // 8 - 1
                    if h == 0:
                        pe.wait_ge(S[f"vband_in{m % 2}"], 16 * 8 * (m // 2 + 1))
                    for a in range(3):
                        vals = vband[:, m % 2, a, hc] if a < 2 else vctx[:, hc]
                        last = mm(out, vals, probT[:, u % 2, a * P:(a + 1) * P], start=(a == 0), stop=(a == 2))
                last.then_inc(S["pv_mm"], 1)

            scores(0)
            for u in range(NU):
                if u + 1 < NU:
                    scores(u + 1)
                prob_turn(u)
                if u >= 1:
                    values(u - 1)
            values(NU - 1)
            barrier(pe, 1)

            pe.wait_ge(S["b_in"], 64)
            for i in range(T):
                for k in range(KC):
                    last = mm(banks[7][:, i * 16:(i + 1) * 16], hT[:, k, tok0[i]:tok0[i] + P], w_ab[:, k, :], start=(k == 0), stop=(k == KC - 1))
            last.then_inc(S["ab_mm"], 1)

            def turn_conv(c):
                pe.wait_ge(S["ys_ready"], c + 1)
                if c >= 2:
                    pe.wait_ge(S["tok_ready"], c - 1)
                elif c == 1:
                    pe.wait_ge(S["gc_used"], 1)
                b = 4 + 2 * (c % 2)
                nc.tensor.transpose(banks[b + 1][:, 0:P], ys[:, c % 2, 0:P], ident)
                for i in range(4):
                    o = SEQ + 2 + i * P
                    last = nc.tensor.transpose(banks[b][:, i * P:(i + 1) * P], ys[:, c % 2, o:o + P], ident)
                last.then_inc(S["tok_mm"], 1)

            for c in range(12):
                name = ("qb", "kb", "vb")[c // 4]
                if c % 4 == 0:
                    w_wait(pe, name)
                if c >= 2:
                    pe.wait_ge(S["xc_ready"], c - 1)
                w = ringv[:, w_slot(name), :, (c % 4) * P:(c % 4 + 1) * P]
                for k in range(KC):
                    mm(banks[2 * (c % 2) + 1][:, 0:SEQ], w[:, k, :], hT[:, k, 0:SEQ], start=(k == 0), stop=(k == KC - 1))
                for k in range(KC):
                    last = mm(banks[2 * (c % 2)][:, :], w[:, k, :], hT[:, k, SEQ:TOK], start=(k == 0), stop=(k == KC - 1))
                last.then_inc(S["cm_mm"], 1)
                if c == 0:
                    pe.wait_ge(S["g_ready"], 1)
                    n = T * H_B
                    mm(banks[7][:, 128:128 + 2 * n], ones, gt[:, 0, 0:2 * n], start=True, stop=True)
                    mm(banks[7][:, 128 + 2 * n:128 + 3 * n], upper, gt[:, 0, 0:n], start=True, stop=True)
                    mm(banks[7][:, 128 + 3 * n:128 + 4 * n], lower, gt[:, 0, n:2 * n], start=True, stop=True).then_inc(S["gc_mm"], 1)
                if c >= 1:
                    turn_conv(c - 1)
            turn_conv(11)
            for i in range(T):
                pe.wait_ge(S["rope_done"], i + 1)
                for g in range(2):
                    if i >= 2:
                        pe.wait_ge(S["kqT_ready"], 2 * (i - 2) + g + 1)
                    elif i == 0:
                        pe.wait_ge(S["xc_ready"], 12)
                    for h in range(H_B):
                        o = g * W_B + h * DK
                        last = nc.tensor.transpose(banks[2 * (i % 2) + g][:, h * P:(h + 1) * P], qkv[:, i, o:o + P], ident)
                    last.then_inc(S["kqT_mm"], 1)

            NL = len(LEVELS)
            pe.wait_ge(S["kqT_ready"], 2 * T)
            pe.wait_ge(S["tok_ready"], 12)
            for p in range(T):
                tile = [0 if p == 0 else (p if d == 0 else T - p) for d in range(2)]
                for d in range(2):
                    U, i = unit[d], tile[d]
                    b = 4 * d
                    if p >= 1:
                        pe.wait_ge(S[f"nwt{d}"], p)
                        pe.wait_ge(S[f"os{d}"], 2 * p)
                    for h in range(H_B):
                        col = (d * T + i) * H_B + h
                        last = mm(banks[b][:, h * P:(h + 1) * P], gt[:, 0, col:col + 1].to_broadcast([P, P]), (upper, lower)[d], start=True, stop=True)
                    last.then_inc(S[f"row_mm{d}"], 1)
                    kd, qd = kdT[:, :, tok0[i]:tok0[i] + P], qdT[:, :, tok0[i]:tok0[i] + P]
                    for h in range(H_B):
                        mm(banks[b + 1][:, h * P:(h + 1) * P], kd[:, h], kd[:, h], start=True, stop=True)
                        last = mm(banks[b + 2][:, h * P:(h + 1) * P], kd[:, h], qd[:, h], start=True, stop=True)
                    last.then_inc(S[f"kq_mm{d}"], 1)
                for n in range(NL):
                    for d in range(2):
                        U = unit[d]
                        b = 4 * d
                        if n == 0:
                            pe.wait_ge(S[f"dpre{d}"], p + 1)
                            pe.wait_ge(S[f"prep{d}"], 2 * p + 1)
                            pe.wait_ge(S[f"bt{d}"], 2 * p + 2)
                        else:
                            pe.wait_ge(S[f"mn{d}"], NL * p + n)
                        pe.wait_ge(S[f"msk{d}"], NL * p + n + 1)
                        for h in range(H_B):
                            last = mm(banks[b][:, h * P:(h + 1) * P], U[f"mask{n % 2}"][:, h], U["inv"][:, h], start=True, stop=True)
                        last.then_inc(S[f"x_mm{d}"], 1)
                    for d in range(2):
                        U = unit[d]
                        b = 4 * d
                        pe.wait_ge(S[f"xs{d}"], NL * p + n + 1)
                        for h in range(H_B):
                            mm(banks[b + 1][:, h * P:(h + 1) * P], U["invT"][:, h], U["xs"][:, h], start=True, stop=True)
                            last = mm(banks[b + 2][:, h * P:(h + 1) * P], U["xs"][:, h], U["invT"][:, h], start=True, stop=True)
                        last.then_inc(S[f"p_mm{d}"], 1)
                for d in range(2):
                    U = unit[d]
                    pe.wait_ge(S[f"mn{d}"], NL * (p + 1))
                    pe.wait_ge(S[f"prep{d}"], 2 * p + 2)
                    for h in range(H_B):
                        last = mm(banks[4 * d][:, h * P:(h + 1) * P], U["kexp"][:, h], U["invT"][:, h], start=True, stop=True)
                    last.then_inc(S[f"wt_mm{d}"], 1)
                for d in range(2):
                    U, i = unit[d], tile[d]
                    pe.wait_ge(S[f"nwt{d}"], p + 1)
                    if p == 1:
                        pe.wait_ge(S["states_in"], 32)
                    if p == 0:
                        pe.wait_ge(S[f"st{d}"], 1)
                    else:
                        pe.wait_ge(S[f"os{d}"], 2 * p)
                    for h in range(H_B):
                        out = banks[4 * d + 1][:, h * P:(h + 1) * P]
                        mm(out, U["invT"][:, h], qkv[:, i, 2 * W_B + h * P:2 * W_B + (h + 1) * P], start=True, stop=False)
                        last = mm(out, U["nwT"][:, h], U["state"][:, h], start=False, stop=True)
                    last.then_inc(S[f"vn_mm{d}"], 1)
                for d in range(2):
                    U = unit[d]
                    pe.wait_ge(S[f"vn{d}"], p + 1)
                    for h in range(H_B):
                        out = banks[4 * d + 3][:, h * P:(h + 1) * P]
                        mm(out, U["erow"][:, h], U["state"][:, h], start=True, stop=False)
                        last = mm(out, U["intraT"][:, h], U["vnew"][:, h], start=False, stop=True)
                    last.then_inc(S[f"o_mm{d}"], 1)
                    for h in range(H_B):
                        last = mm(banks[4 * d + 2][:, h * P:(h + 1) * P], U["kend"][:, h], U["vnew"][:, h], start=True, stop=True)
                    last.then_inc(S[f"o_mm{d}"], 1)
            barrier(pe, 2)

            def turn_ob(i):
                pe.wait_ge(S["ob_ready"], i + 1)
                if i >= 2:
                    pe.wait_ge(S["obT_ready"], i - 1)
                for a in range(4):
                    last = nc.tensor.transpose(banks[4 + i % 2][:, a * P:(a + 1) * P], o_acc[:, i, a * P:(a + 1) * P], ident)
                last.then_inc(S["obT_mm"], 1)

            w_wait(pe, "zb")
            for i in range(T):
                if i >= 2:
                    pe.wait_ge(S["zs_ready"], i - 1)
                rows_mm(banks[i % 2][:, :], "zb", i).then_inc(S["z_mm"], 1)
                if i >= 1:
                    turn_ob(i - 1)
            turn_ob(T - 1)
            pe.wait_ge(S["zs_ready"], T)
            for j in range(4, 12):
                mod_mm(j)
                if j >= 5:
                    mod_bc(j - 1)
            mod_bc(11)
            pe.wait_ge(S["obT_ready"], T)
            pe.wait_ge(S["bc_done"], 24)
            for u in range(NHALF * T):
                n, i = u // T, u % T
                b = 4 * (u % 2)
                if i == 0:
                    for name in (f"proj{n}", f"ga{n}", f"gb{n}"):
                        w_wait(pe, name)
                if u >= 2:
                    pe.wait_ge(S["merged_ready"], u - 1)
                w = ringv[:, w_slot(f"proj{n}")]
                for k in range(4):
                    mm(banks[b][:, :], oaT[:, k, tok0[i]:tok0[i] + P], w[:, k, :], start=(k == 0), stop=(k == 3))
                for k in range(4):
                    mm(banks[b + 1][:, :], obT[:, k, tok0[i]:tok0[i] + P], w[:, 4 + k, :], start=(k == 0), stop=(k == 3))
                rows_mm(banks[b + 2][:, :], f"ga{n}", i)
                rows_mm(banks[b + 3][:, :], f"gb{n}", i).then_inc(S["merge_mm"], 1)
            pe.wait_ge(S["merged_ready"], NHALF * T)
            for i in range(T):
                for g in range(2):
                    if i >= 1:
                        pe.wait_ge(S["mT_ready"], 2 * i - 1 + g)
                    for a in range(4):
                        k = 4 * g + a
                        last = nc.tensor.transpose(banks[4 + g][:, a * P:(a + 1) * P], merged[:, i, k * P:(k + 1) * P], ident)
                    last.then_inc(S["mT_mm"], 1)
            pe.wait_ge(S["mT_ready"], 2 * T)
            for u in range(NHALF * T):
                n, i = u // T, u % T
                if i == 0:
                    w_wait(pe, f"out{n}")
                if u >= 4:
                    pe.wait_ge(S["x2_ready"], u - 3)
                rows_mm(banks[u % 4][:, :], f"out{n}", i).then_inc(S["out_mm"], 1)
            turns(1, h2_tok)
            pe.wait_ge(S["hT_ready"], 4 * T)
            pe.wait_ge(S["b_in"], 80)
            pe.wait_ge(S["x2_ready"], NHALF * T)
            for i in range(T):
                for k in range(KC):
                    last = mm(banks[0][:, i * 36:(i + 1) * 36], hT[:, k, tok0[i]:tok0[i] + P], w_router[:, k, :], start=(k == 0), stop=(k == KC - 1))
            last.then_inc(S["logit_mm"], 1)
            barrier(pe, 3)

            def turn_hid(u):
                pe.wait_ge(S["hid_ready"], u + 1)
                if u >= 2:
                    pe.wait_ge(S["hidT_ready"], u - 1)
                for a in range(2):
                    last = nc.tensor.transpose(banks[2 + u % 2][:, a * P:(a + 1) * P], hid[:, u % 2, a * P:(a + 1) * P], ident)
                last.then_inc(S["hidT_mm"], 1)

            def down(u):
                e = u // T
                pe.wait_ge(S["hidT_ready"], u + 1)
                b = 4 + 2 * (u % 2)
                if u >= 2:
                    pe.wait_ge(S["acc_done"], u - 1)
                for n in range(NHALF):
                    for k in range(2):
                        last = mm(banks[b + n][:, :], hidT[:, u % 2, k * P:(k + 1) * P], edown[e % 2][:, k, n * HALF:(n + 1) * HALF],
                                  start=(k == 0), stop=(k == 1))
                last.then_inc(S["down_mm"], 1)

            for u in range(N_EXPERTS * T):
                e, i = u // T, u % T
                if i == 0:
                    pe.wait_ge(S[f"e_in{e % 2}"], 32 * (e // 2 + 1))
                if u >= 2:
                    pe.wait_ge(S["hid_ready"], u - 1)
                for k in range(KC):
                    last = mm(banks[u % 2][:, :], hT[:, k, tok0[i]:tok0[i] + P], eup[e % 2][:, k, :], start=(k == 0), stop=(k == KC - 1))
                last.then_inc(S["eup_mm"], 1)
                if u >= 1:
                    turn_hid(u - 1)
                    if u >= 2:
                        down(u - 2)
            turn_hid(N_EXPERTS * T - 1)
            down(N_EXPERTS * T - 2)
            down(N_EXPERTS * T - 1)


_OUTS = [("y", (T, P, D)), ("new_k", (P, W_A)), ("new_v", (P, W_A)), ("new_state", (2, P, H_B, P))]


def layout(i):
    f = {k: np.asarray(v) for k, v in i.items()}

    def blocked(w, cols=HALF):
        k, n = w.shape
        return w.reshape(k // P, P, n // cols, cols).transpose(2, 1, 0, 3).reshape(n // cols, P, -1)

    a = {}
    a["x"] = np.concatenate([f["x_prompt"][0], f["x_sample"][0]]).reshape(T, P, D)
    a["cT"] = np.stack([f["c_ctx"], f["c"][0]], axis=1).reshape(KC, P, 2).transpose(1, 0, 2).reshape(P, -1)
    wi = f["w_in"][0]
    mod, win = blocked(f["w_mod"][0]), blocked(np.concatenate([wi[:, :3584], wi[:, 3600:]], axis=1))
    proj = blocked(np.concatenate([f["w_proj_a"][0], f["w_proj_b"][0]], axis=0))
    out = blocked(f["w_out"][0])
    by_name = {f"mod{j}": mod[j] for j in range(12)}
    for n, name in enumerate(["qa", "ka", "va", "qb", "kb", "vb", "zb", "ga0", "ga1", "gb0", "gb1"]):
        by_name[name] = win[n]
    for n in range(2):
        by_name[f"proj{n}"], by_name[f"out{n}"] = proj[n], out[n]
    a["w_blocks"] = np.stack([by_name[name] for name in BLOCKS])
    a["w_ab"] = blocked(wi[:, 3584:3600], 16)[0]
    a["bmod"] = np.broadcast_to(f["b_mod"].reshape(1, 12, HALF), (2, 12, HALF))
    a["norm_w"] = np.broadcast_to(np.stack([f["norm1_w"][0], f["norm2_w"][0]])[None], (2, 2, D))
    row = np.concatenate([f["q_norm_w"][0], f["k_norm_w"][0], f["o_norm_w"][0], f["b_router_g"][0], f["b_router_e"][0],
                          f["dt_bias"][0].reshape(-1), f["a_log"][0].reshape(-1), np.arange(8, 0, -1, dtype=np.float32)])
    a["rows"] = np.broadcast_to(row, (P, R_ALL))
    a["conv_w"] = f["conv_w"][0].reshape(CONV_K, 12, P).transpose(2, 1, 0).reshape(P, -1)
    a["w_router"] = blocked(np.concatenate([f["w_router_g"][0], f["w_router_e"][0]], axis=1), 36)[0]
    a["w_up"] = np.stack([blocked(np.concatenate([f["w_exp_gate"][0, e], f["w_exp_up"][0, e]], axis=1))[0] for e in range(N_EXPERTS)])
    a["w_down"] = np.stack([blocked(f["w_exp_down"][0, e], D)[0] for e in range(N_EXPERTS)])
    a["kctx"] = f["cache_attn_k"].reshape(P, W_A)
    a["vctx"] = f["cache_attn_v"].reshape(P, W_A)
    a["state0"] = np.stack([f["state_delta_fwd"][0, 0], f["state_delta_bwd"][0, 0]]).transpose(0, 2, 1, 3).reshape(2, P, -1)
    rpb = f["rpb"][0]
    r, q, kr, k = (x.reshape(s) for x, s in ((np.arange(ROWS), (-1, 1, 1, 1)), (np.arange(QB_W), (1, -1, 1, 1)),
                                             (np.arange(ROWS), (1, 1, -1, 1)), (np.arange(BAND_W), (1, 1, 1, -1))))
    bias = np.zeros((3, P, H_A, KEYS), rpb.dtype)
    for m in (0, 1, 3):
        q_col, k_col = m * QB_W + q, BAND_START[m] + k
        start = np.clip(q_col - WIN_W // 2, 0, GRID_W - WIN_W)
        seen = (k_col >= start) & (k_col < start + WIN_W) & (kr >= 0) & (r >= 0)
        at = rpb[:, kr - r + WIN_H - 1 + 0 * q + 0 * k, np.clip(k_col - q_col + WIN_W - 1, 0, 2 * WIN_W - 2) + 0 * kr + 0 * r]
        at = np.where(seen[None], at, np.float32(-BIG))
        bias[BIAS_OF[m], :, :, :BAND] = at.reshape(H_A, P, BAND).transpose(1, 0, 2)
    a["bias"] = bias.reshape(3, P, -1)
    a["const"], a["level_mask"] = constants()
    pos = np.arange(DEC_SEQ)
    inv = 10000.0 ** (-np.arange(DK // 4, dtype=np.float32) / (DK // 4))
    ang = np.concatenate([(pos // GRID_W)[:, None] * inv, (pos % GRID_W)[:, None] * inv], axis=1).astype(np.float32)
    a["rope"] = np.stack([np.cos(ang), np.sin(ang)], axis=1).reshape(4, P, 2, 64).transpose(1, 0, 2, 3).reshape(P, -1).astype(np.float32)
    return a


def kernel(**inputs):
    import concourse.bacc as bacc
    from concourse.bass_utils import run_bass_kernel_spmd

    nc = bacc.Bacc("TRN2", target_bir_lowering=False, num_devices=1)
    arrays, t = {}, {}
    for name, a in layout(inputs).items():
        if name == "level_mask":
            a = a.astype(mybir.dt.np(BF16))
        a = np.ascontiguousarray(a)
        arrays[f"in_{name}"] = a
        t[name] = nc.dram_tensor(f"in_{name}", a.shape, mybir.dt.from_np(a.dtype), kind="ExternalInput").ap()
    for name, shape in _OUTS:
        t[name] = nc.dram_tensor(f"out_{name}", shape, F32, kind="ExternalOutput").ap()
    t["v_scratch"] = nc.dram_tensor("v_scratch", (T - 1, P, W_A), F32, kind="Internal").ap()
    build(nc, t)
    r = run_bass_kernel_spmd(nc, [arrays], core_ids=[0]).results[0]
    y = r["out_y"].reshape(TOK, D)
    state = r["out_new_state"].transpose(0, 2, 1, 3).reshape(2, 1, 1, H_B, DK, DK)
    return (y[:SEQ].reshape(1, SEQ, D), y[SEQ:].reshape(1, DEC_SEQ, D), r["out_new_k"].reshape(1, 1, SEQ, H_A, D_HA),
            r["out_new_v"].reshape(1, 1, SEQ, H_A, D_HA), state[0], state[1])
```

```python
from contextlib import ExitStack

import numpy as np

import concourse.bass as bass
from concourse import mybir

F32 = mybir.dt.float32
I32 = mybir.dt.int32
BF16 = mybir.dt.bfloat16
ALU = mybir.AluOpType
ACT = mybir.ActivationFunctionType
AX_X = mybir.AxisListType.X

P = 128
D = 1024
KC = D // P
SEQ, DEC_SEQ, PAST = 128, 512, 128
TOK = SEQ + DEC_SEQ
T = TOK // P
GRID_W, ROWS = 64, DEC_SEQ // 64
H_A, D_HA, W_A = 8, 64, 512
WIN_H, WIN_W, QB_W, BAND_W = 8, 16, 16, 32
N_CB = GRID_W // QB_W
BAND = ROWS * BAND_W
KEYS = BAND + PAST
BAND_START = [min(max(m * QB_W - WIN_W // 2, 0), GRID_W - BAND_W) for m in range(N_CB)]
BIAS_OF = [0, 1, 1, 2]
H_B, DK, W_B = 4, 128, 512
CONV_K = 5
LEVELS = [1, 2, 4, 8, 16, 32, 64]
N_GROUPS, EXP_PER_GROUP = 4, 8
N_EXPERTS = N_GROUPS * EXP_PER_GROUP
D_FF = 256
CAP = P
NOWHERE = 1 << 20
EPS = 1e-6
BIG = 1e30
HALF = 512
NHALF = D // HALF
XC = 2 + SEQ + 2 + DEC_SEQ + 2
YC = XC - CONV_K + 1

BLOCKS = (["mod0", "mod1", "mod2", "mod3", "qa", "ka", "va", "qb", "kb", "vb", "zb"]
          + [f"mod{j}" for j in range(4, 12)]
          + ["proj0", "ga0", "gb0", "proj1", "ga1", "gb1", "out0", "out1"])
BLOCK = {name: n for n, name in enumerate(BLOCKS)}
RING = 3

C_IDENT, C_UP, C_LOW, C_ONES, C_SLOW = (n * P for n in range(5))
C_NEG = 5 * P
C_SEL = 7 * P
C_F32 = 9 * P
R_QN, R_KN, R_ON, R_BR, R_DT, R_AL, R_FIRST = 0, 64, 128, 256, 292, 300, 308
R_IOTA = R_FIRST + EXP_PER_GROUP
R_ALL = R_IOTA + N_EXPERTS


def constants():
    i = np.arange(P)
    up = (i[:, None] <= i[None, :]).astype(np.float32)
    low = up.T.copy()
    slow = (i[:, None] < i[None, :]).astype(np.float32)
    neg = [(1 - up) * -BIG, (1 - low) * -BIG]
    sel = np.zeros((P, 2, P), np.float32)
    sel[0, 0], sel[1, 1] = 1, 1
    c = np.concatenate([np.eye(P, dtype=np.float32), up, low, np.ones((P, P), np.float32), slow, *neg,
                        sel.reshape(P, -1)], axis=1).astype(np.float32)
    lv = []
    for d in range(2):
        for n in LEVELS:
            b = i // n
            m = (b[None, :] % 2 == 1) & (b[:, None] == b[None, :] - 1)
            lv.append((m if d == 0 else m.T).astype(np.float32))
    return c, np.concatenate(lv, axis=1)


def build(nc, t):
    with ExitStack() as ctx:
        arena = ctx.enter_context(nc.sbuf_tensor("arena", [P, 53000], F32))
        banks = [ctx.enter_context(nc.psum_tensor(f"bank{n}", [P, HALF], F32)) for n in range(8)]
        sems = {}

        def sem(name):
            sems[name] = ctx.enter_context(nc.semaphore(name))
            return sems[name]

        top = [0]

        def cut(*shape):
            n = int(np.prod(shape))
            v = arena[:, top[0]:top[0] + n]
            top[0] += n
            assert top[0] <= 53000, top[0]
            if len(shape) == 2:
                v = v.rearrange("p (a b) -> p a b", a=shape[0])
            if len(shape) == 3:
                v = v.rearrange("p (a b c) -> p a b c", a=shape[0], b=shape[1])
            if len(shape) == 4:
                v = v.rearrange("p (a b c d) -> p a b c d", a=shape[0], b=shape[1], c=shape[2])
            return v

        const = cut(C_F32)
        ident, upper, lower = (const[:, o:o + P] for o in (C_IDENT, C_UP, C_LOW))
        ones, earlier = const[:, C_ONES:C_ONES + P], const[:, C_SLOW:C_SLOW + P]
        negmask = [const[:, C_NEG + d * P:C_NEG + (d + 1) * P] for d in range(2)]
        pick = [const[0:2, C_SEL + c * P:C_SEL + (c + 1) * P] for c in range(2)]
        rows = cut(R_ALL)
        cT = cut(KC * 2)
        silu_cT = cut(KC, 2)
        mod_row = cut(2, HALF)
        stat = cut(2, T)
        eps_col = cut(1)
        nowhere = cut(2 * N_EXPERTS).bitcast(I32)
        ring = cut(RING, KC * HALF)
        ringv = ring.rearrange("p s (k n) -> p s k n", k=KC)
        hT = cut(KC, TOK)
        oa_at = top[0]
        oaT = cut(H_A // 2, TOK)
        shared = top[0]
        shift_bc = cut(2, D)
        scale_bc = cut(2, D)
        low_end = top[0]

        x_sb = cut(T, D)
        h_tok = cut(2, D)
        bmod_a = cut(4, HALF)
        norm_a = cut(D)
        norm_end = top[0]
        top[0] = low_end
        bias = cut(2, H_A, KEYS)
        vband = cut(2, 2, W_A)
        assert top[0] <= norm_end
        top[0] = norm_end
        qaT = cut(H_A // 2, TOK)
        qa_blocks = qaT[:, :, SEQ:TOK].rearrange("p a (m r c) -> p a m r c", m=N_CB, r=ROWS)
        kaT = cut(H_A // 2, TOK)
        va0 = cut(W_A)
        vctx = cut(W_A)
        kctx = cut(W_A)
        kctxT = cut(H_A // 2, PAST)
        square = cut(2, W_A)
        qk_tok = cut(2, W_A)
        va_out = cut(2, W_A)
        headstat = cut(2, 3 * H_A)
        score = cut(2, KEYS)
        probT = cut(2, KEYS)
        sstat = cut(2, 3)

        top[0] = low_end
        o_acc = cut(T, W_B)
        phase_c = top[0]
        level_mask = cut(2 * len(LEVELS) * P // 2).bitcast(BF16).rearrange("p (d n c) -> p d n c", d=2, n=len(LEVELS))
        rope = cut(4, 2, 64)
        conv_w = cut(12, CONV_K)
        w_ab = cut(KC, 16)
        ab = cut(T, 16)
        gt = cut(12, 2 * T * H_B)
        qkstat = cut(T, 16)
        qkv = cut(T, 3 * W_B)
        kdT = cut(H_B, TOK)
        qdT = cut(H_B, TOK)
        phase_b = top[0]
        xc = cut(2, XC)
        yc = cut(2, YC)
        ys = cut(2, YC)
        sq_b = cut(2, 2 * W_B)
        ropet = cut(4, 2 * H_B, 64)
        top[0] = phase_b
        unit = [{}, {}]
        for k in ("decayT", "gramT", "intraT", "mask0", "mask1", "xs", "inv", "invT"):
            unit[0][k] = cut(H_B, P)
            unit[1][k] = cut(H_B, P)
        top[0], back = shared, top[0]
        for k in ("erow", "kexp", "kend", "state"):
            unit[0][k] = cut(H_B, P)
            unit[1][k] = cut(H_B, P)
        top[0] = back
        for U in unit:
            U["nwT"] = U["mask0"]
            U["vnew"] = U["xs"]

        top[0] = phase_c
        gate1_bc = cut(2, D)
        gate2_bc = cut(2, D)
        osq = cut(2, W_B)
        ostat = cut(T, 8)
        zs = cut(2, W_B)
        obT = cut(H_B, TOK)
        sga = cut(2, HALF)
        sgb = cut(2, HALF)
        merged = cut(T, D)
        w_router = cut(KC, N_GROUPS + N_EXPERTS)
        combine = cut(T, N_EXPERTS)
        x2 = cut(T, D)
        logit = cut(T, N_GROUPS + N_EXPERTS)
        ex = cut(2, T, 5)
        gmax = cut(T, 1)
        gsel = cut(T, N_GROUPS)
        geq = cut(T, N_GROUPS)
        eprod = cut(T, N_GROUPS, EXP_PER_GROUP)
        ingrp = cut(T, EXP_PER_GROUP)
        eeq = cut(T, EXP_PER_GROUP)
        esel = cut(2, T, EXP_PER_GROUP)
        emax = cut(3, T, 1)
        wts = cut(3, T, 1)
        chosen = cut(2, T, N_EXPERTS)
        picked = cut(T, N_EXPERTS)
        place = cut(T, N_EXPERTS)
        ecount = cut(N_EXPERTS)
        most = cut(1)
        dest = cut(2, T)
        dest_i = cut(2, T).bitcast(I32)
        dense = cut(1).bitcast(I32)
        payload = cut(2 * T * 2).bitcast(I32).rearrange("p (r t n) -> p r t n", r=2, t=T)
        end = top[0]
        top[0] = phase_c + 2 * 2 * D + 2 * W_B + T * 8 + 2 * W_B
        h2_tok = cut(2, D)
        top[0] = phase_c + 2 * 2 * D + 4 * W_B + T * 8 + H_B * TOK + 4 * HALF
        bmod_c = cut(8, HALF)
        norm_c = cut(D)
        top[0] = end
        flat = lambda v: v.rearrange("p a b -> p (a b)")
        eup = [ringv[:, n] for n in range(3)]
        edown = [flat(merged)[:, n * 2 * D:(n + 1) * 2 * D].rearrange("p (k n) -> p k n", k=2) for n in range(2)] + [gate1_bc]
        sg, hid, hidT = sga, zs, osq
        rows_in = [shift_bc[:, 0], shift_bc[:, 1], scale_bc[:, 0], scale_bc[:, 1]]
        rowsT = [flat(hT)[:, n * D:(n + 1) * D].rearrange("p (k n) -> p k n", k=KC) for n in range(2)]
        rows_out = [flat(hT)[:, (2 + n) * D:(3 + n) * D] for n in range(3)]
        slots = flat(merged)[:, 4 * D:4 * D + 2 * N_EXPERTS].bitcast(I32).rearrange("p (e n) -> p e n", n=2)
        acc = arena[:, oa_at:oa_at + T * D].rearrange("p (t n) -> p t n", t=T)

        for n in ("consts_in", "kv_ctx_in", "b_in", "states_in", "c_in", "bias_in0", "bias_in1", "vband_in0", "vband_in1",
                  "silu_c", "mod_mm", "row_ready", "bc_mm", "bc_done", "ssq_ready", "h_ready",
                  "hT_mm", "hT_ready", "proj_mm", "squared", "headsum", "headstd", "qk_ready", "qkT_mm",
                  "qkT_ready", "va_ready", "kctxT_mm", "kctxT_ready", "k_out",
                  "score_mm", "max_ready", "exp_done", "prob_ready", "probT_mm", "probT_ready", "pv_mm", "pv_used",
                  "ab_mm", "g_raw", "g_act", "g_ready", "gc_mm", "gc_used", "gexp_done",
                  "cm_mm", "xc_ready", "conv_ready", "ys_ready", "tok_mm", "tok_ready", "sq_ready", "qksum", "qkstd",
                  "rope_done", "kqT_mm", "kqT_ready", "phase", "pads",
                  "osq_ready", "osum", "ostd", "z_mm", "zs_ready", "ob_ready", "obT_mm", "obT_ready",
                  "merge_mm", "sig_ready", "merged_ready", "mT_mm", "y_out", "mT_ready", "out_mm", "x2_ready",
                  "logit_mm", "router_exp_in", "router_exp",
                  "eup_mm", "silu_done", "hid_ready", "hidT_mm", "hidT_ready", "down_mm", "acc_done", "y_ready",
                  
                  "dve_step", "act_step", "pool_step"):
            sem(n)
        for d in range(2):
            for n in ("row_mm", "kq_mm", "x_mm", "p_mm", "wt_mm", "vn_mm", "o_mm", "erow", "dexp", "xs", "nwt", "dpre",
                      "bt", "mn", "vn", "os", "prep", "msk", "st"):
                sem(f"{n}{d}")
        for s in range(RING):
            sem(f"w_in{s}")
        for s in range(2):
            sem(f"v_scratch{s}")
        for s in range(T):
            sem(f"x_in{s}")
        for n in range(3):
            sem(f"expert_out{n}")
        for n in range(4):
            sem(f"rows_in{n}")
        for n in range(2):
            sem(f"h2_out{n}")
        for n in ("chosen_ready", "place_mm", "dest_ready", "dense_ready", "table","rowsT_mm",
                  "rowsT_ready", "rows_clear",
                  "rowsT_ready2", "s_out2", "weighted"):
            sem(n)
        S = sems

        def w_slot(name):
            return BLOCK[name] % RING

        def w_wait(eng, name):
            eng.wait_ge(S[f"w_in{w_slot(name)}"], 16 * (BLOCK[name] // RING + 1))

        def expert_loaded(e):
            return 16 * len(range(e % 3, len(BLOCKS), RING)) + 32 * (e // 3 + 1)

        def read_by(name):
            kind, n = name[:-1], name[-1]
            if kind == "mod":
                return S["mod_mm"], int(name[3:]) + 1
            if name[:3] == "mod":
                return S["mod_mm"], int(name[3:]) + 1
            if name in ("qa", "ka", "va"):
                return S["proj_mm"], T * (("qa", "ka", "va").index(name) + 1)
            if name in ("qb", "kb", "vb"):
                return S["cm_mm"], 4 * (("qb", "kb", "vb").index(name) + 1)
            if name == "zb":
                return S["z_mm"], T
            if kind in ("proj", "ga", "gb"):
                return S["merge_mm"], T * (int(n) + 1)
            return S["out_mm"], T * (int(n) + 1)

        def stepper(eng, own, counts):

            def step(ins, signal=own):
                counts[signal] = counts.get(signal, 0) + 1
                ins.then_inc(S[signal], 1)
                eng.wait_ge(S[signal], counts[signal])

            return step

        def barrier(eng, n):
            eng.drain().then_inc(S["phase"], 1)
            eng.wait_ge(S["phase"], 4 * n)

        tok0 = [i * P for i in range(T)]
        block = ctx.enter_context(nc.Block())

        @block.sync
        def _(sp):
            sp.dma_start(cT, t["cT"]).then_inc(S["c_in"], 16)
            for n, name in enumerate(BLOCKS):
                if n >= RING:
                    sp.wait_ge(*read_by(BLOCKS[n - RING]))
                sp.dma_start(ring[:, n % RING, :], t["w_blocks"][n]).then_inc(S[f"w_in{n % RING}"], 16)
            def expert_in(e):
                sp.dma_start(eup[e % 3], t["w_up"][e].rearrange("p (k n) -> p k n", k=KC)).then_inc(S[f"w_in{e % 3}"], 16)
                sp.dma_start(edown[e % 3], t["w_down"][e].rearrange("p (k n) -> p k n", k=2)).then_inc(S[f"w_in{e % 3}"], 16)

            sp.wait_ge(*read_by("gb1"))
            sp.wait_ge(S["mT_mm"], 2 * T)
            expert_in(0)
            sp.wait_ge(*read_by("out0"))
            expert_in(1)
            sp.wait_ge(*read_by("out1"))
            sp.wait_ge(S["x2_ready"], NHALF * T)
            expert_in(2)
            sp.wait_ge(S["dense_ready"], 1)
            is_dense = sp.value_load(dense[0:1, 0:1])
            with sp.If(is_dense > 0):
                for e in range(3, N_EXPERTS):
                    sp.wait_ge(S["down_mm"], T * (e - 2))
                    expert_in(e)
            with sp.Else():
                for e in range(3, N_EXPERTS):
                    sp.wait_ge(S["down_mm"], e - 2)
                    expert_in(e)
                for n in range(3):
                    sp.wait_ge(S[f"expert_out{n}"], 16 * len(range(n, N_EXPERTS, 3)))
                for i in range(T):
                    if i >= 2:
                        sp.wait_ge(S["y_ready"], i - 1)
                    for r in range(2):
                        sp.dma_start(rows_in[2 * (i % 2) + r], t["y_scratch"][(r * T + i) * P:(r * T + i + 1) * P, :])\
                          .then_inc(S[f"w_in{i % 2}"], 16)
            for i in range(T):
                sp.wait_ge(S["y_ready"], i + 1)
                sp.dma_start(t["y"][i], x2[:, i, :]).then_inc(S["y_out"], 16)
            sp.wait_ge(S["y_out"], 16 * T)

        @block.gpsimd
        def _(pool):
            step = stepper(pool, "pool_step", {})
            step(pool.memset(nowhere, NOWHERE))
            pool.dma_start(t["slot_table"].rearrange("(r e) n -> r (e n)", e=N_EXPERTS), nowhere).then_inc(S["table"], 16)
            pool.dma_start(const, t["const"]).then_inc(S["consts_in"], 16)
            pool.dma_start(rows, t["rows"]).then_inc(S["consts_in"], 16)
            pool.dma_start(bmod_a[0:2], t["bmod"][:, 0:4]).then_inc(S["consts_in"], 16)
            pool.dma_start(norm_a[0:2], t["norm_w"][:, 0]).then_inc(S["consts_in"], 16)
            for i in range(T):
                pool.dma_start(x_sb[:, i, :], t["x"][i]).then_inc(S[f"x_in{i}"], 16)
            pool.dma_start(kctx, t["kctx"]).then_inc(S["kv_ctx_in"], 16)
            pool.dma_start(vctx, t["vctx"]).then_inc(S["kv_ctx_in"], 16)
            pool.wait_ge(S["hT_ready"], 2 * T)
            for u in range(2):
                pool.dma_start(bias[:, u], t["bias"][u].rearrange("p (h k) -> p h k", h=H_A)).then_inc(S[f"bias_in{u}"], 16)
            pool.wait_ge(S["qk_ready"], T + 1)
            pool.dma_start(t["new_k"], qk_tok[:, T % 2, :]).then_inc(S["k_out"], 16)
            pool.wait_ge(S["va_ready"], 1)
            pool.dma_start(t["new_v"], va0).then_inc(S["k_out"], 16)
            for i in range(1, T):
                pool.wait_ge(S["va_ready"], i + 1)
                pool.dma_start(t["v_scratch"][i - 1], va_out[:, i % 2, :]).then_inc(S[f"v_scratch{i % 2}"], 16)
            for s in range(2):
                pool.wait_ge(S[f"v_scratch{s}"], 16 * (T - 1) // 2)
            grid = t["v_scratch"].rearrange("i (r c) d -> (i r) c d", c=GRID_W)
            for m in range(N_CB):
                if m >= 2:
                    pool.wait_ge(S["pv_mm"], 8 * m)
                for j in range(2):
                    for r in range(4):
                        pool.dma_start(vband[r * BAND_W:(r + 1) * BAND_W, m % 2, j, :],
                                       grid[4 * j + r, BAND_START[m]:BAND_START[m] + BAND_W, :]).then_inc(S[f"vband_in{m % 2}"], 16)
                if m == 3:
                    pool.dma_start(bias[:, 0], t["bias"][2].rearrange("p (h k) -> p h k", h=H_A)).then_inc(S["bias_in0"], 16)
            pool.wait_ge(S["k_out"], 32)
            barrier(pool, 1)

            pool.dma_start(level_mask, t["level_mask"].rearrange("p (d n c) -> p d n c", d=2, n=len(LEVELS))).then_inc(S["b_in"], 16)
            pool.dma_start(rope, t["rope"].rearrange("p (a b c) -> p a b c", a=4, b=2)).then_inc(S["b_in"], 16)
            pool.dma_start(conv_w, t["conv_w"].rearrange("p (a b) -> p a b", a=12)).then_inc(S["b_in"], 16)
            pool.dma_start(w_ab, t["w_ab"].rearrange("p (a b) -> p a b", a=KC)).then_inc(S["b_in"], 16)
            pool.wait_ge(S["gexp_done"], 1)
            pool.wait_ge(S["kqT_ready"], 2 * T)
            pool.wait_ge(S["b_in"], 64)
            for p in range(T):
                for d in range(2):
                    U = unit[d]
                    i = 0 if p == 0 else (p if d == 0 else T - p)
                    if p == 1:
                        if d == 0:
                            pool.wait_ge(S["states_in"], 32)
                        pool.dma_start(U["state"], t["state0"][d].rearrange("p (h c) -> p h c", h=H_B)).then_inc(S["states_in"], 16)
                    if p >= 1:
                        pool.wait_ge(S[f"o_mm{d}"], 2 * p)
                    col = (d * T + i) * H_B
                    step(pool.tensor_tensor(U["inv"], ident.unsqueeze(1).to_broadcast([P, H_B, P]),
                                            gt[:, 3, col:col + H_B].unsqueeze(2).to_broadcast([P, H_B, P]), ALU.mult))
                    step(pool.tensor_copy(U["invT"], U["inv"]), f"prep{d}")
                    k_i = qkv[:, i, W_B:2 * W_B].rearrange("p (h c) -> p h c", h=H_B)
                    step(pool.tensor_tensor(U["kexp"], k_i, gt[:, 4, col:col + H_B].unsqueeze(2).to_broadcast([P, H_B, P]), ALU.mult))
                    step(pool.tensor_tensor(U["kend"], k_i, gt[:, 5, col:col + H_B].unsqueeze(2).to_broadcast([P, H_B, P]), ALU.mult))
                    pool.wait_ge(S[f"erow{d}"], p + 1)
                    step(pool.tensor_tensor(U["erow"], U["erow"], qdT[:, :, tok0[i]:tok0[i] + P], ALU.mult), f"prep{d}")
                for n in range(len(LEVELS)):
                    for d in range(2):
                        U = unit[d]
                        if n == 0:
                            pool.wait_ge(S[f"bt{d}"], 2 * p + 1)
                        if n >= 2:
                            pool.wait_ge(S[f"x_mm{d}"], len(LEVELS) * p + n - 1)
                        step(pool.tensor_tensor(U[f"mask{n % 2}"], U["gramT"],
                                                level_mask[:, d, n, :].unsqueeze(1).to_broadcast([P, H_B, P]), ALU.mult), f"msk{d}")
                if p == 0:
                    for d in range(2):
                        pool.wait_ge(S[f"os{d}"], 2)
                        pool.dma_start(t["new_state"][d], unit[d]["state"]).then_inc(S["states_in"], 16)
            barrier(pool, 2)
            pool.dma_start(bmod_c[0:2], t["bmod"][:, 4:12]).then_inc(S["b_in"], 16)
            pool.dma_start(norm_c[0:2], t["norm_w"][:, 1]).then_inc(S["b_in"], 16)
            pool.dma_start(w_router, t["w_router"].rearrange("p (a b) -> p a b", a=KC)).then_inc(S["b_in"], 16)
            for i in range(T):
                pool.dma_start(x2[:, i, :], t["x"][i]).then_inc(S[f"x_in{i}"], 16)
            for i in range(T):
                pool.wait_ge(S[f"x_in{i}"], 32)
            pool.dma_start(payload, t["payload"].rearrange("p (r t n) -> p r t n", r=2, t=T)).then_inc(S["b_in"], 16)
            barrier(pool, 3)

            pool.wait_ge(S["table"], 16)
            pool.wait_ge(S["b_in"], 128)
            for n in range(2):
                pool.wait_ge(S[f"h2_out{n}"], 16 * len(range(n, T, 2)))
            pool.wait_ge(S["dense_ready"], 1)
            is_dense = pool.value_load(dense[0:1, 0:1])
            with pool.If(is_dense <= 0):
                pool.wait_ge(S["dest_ready"], 1)
                for r in range(2):
                    for i in range(T):
                        pool.indirect_dma_start(out=t["slot_table"], out_offset=bass.IndirectOffsetOnAxis(ap=dest_i[:, r, i:i + 1], axis=0),
                                                in_=payload[:, r, i, :], in_offset=None,
                                                bounds_check=CAP * N_EXPERTS - 1, oob_is_err=False).then_inc(S["table"], 16)
                pool.wait_ge(S["table"], 16 * (1 + 2 * T))
                pool.dma_start(slots, t["slot_table"].rearrange("(r e) n -> r e n", e=N_EXPERTS)).then_inc(S["table"], 16)
                pool.wait_ge(S["table"], 16 * (2 + 2 * T))
                pool.wait_ge(S["rows_clear"], 1)
                for e in range(N_EXPERTS + 3):
                    if e < N_EXPERTS:
                        if e >= 4:
                            pool.wait_ge(S["rowsT_mm"], 2 * (e - 3))
                        pool.indirect_dma_start(out=rows_in[e % 4], out_offset=None, in_=t["h_scratch"],
                                                in_offset=bass.IndirectOffsetOnAxis(ap=slots[:, e, 0:1], axis=0),
                                                bounds_check=TOK - 1, oob_is_err=False).then_inc(S[f"rows_in{e % 4}"], 16)
                    if e >= 3:
                        o = e - 3
                        pool.wait_ge(S["acc_done"], o + 1)
                        pool.wait_ge(S["s_out2"], o + 1)
                        pool.indirect_dma_start(out=t["y_scratch"], out_offset=bass.IndirectOffsetOnAxis(ap=slots[:, o, 1:2], axis=0),
                                                in_=rows_out[o % 3], in_offset=None,
                                                bounds_check=2 * TOK - 1, oob_is_err=False).then_inc(S[f"expert_out{o % 3}"], 16)

        @block.scalar
        def _(act):
            steps = {}
            step = stepper(act, "act_step", steps)
            sc = nc.scalar
            act.wait_ge(S["c_in"], 16)
            step(sc.activation(silu_cT, cT.rearrange("p (a b) -> p a b", a=KC), ACT.Silu), "silu_c")

            def bc_copy(j):
                dst = {0: shift_bc, 1: scale_bc, 2: gate1_bc, 3: shift_bc, 4: scale_bc, 5: gate2_bc}[j // 2]
                for c in range(2):
                    act.wait_ge(S["bc_mm"], 2 * j + c + 1)
                    step(sc.activation(dst[:, c, (j % 2) * HALF:(j % 2 + 1) * HALF], banks[2 + c][:, :], ACT.Copy), "bc_done")

            def norm_act(n, x):
                for i in range(T):
                    if n == 0:
                        act.wait_ge(S[f"x_in{i}"], 16)
                    else:
                        act.wait_ge(S["x2_ready"], T * NHALF)
                    step(sc.activation(hT[:, 0:2, 0:HALF], x[:, i, :].rearrange("p (a b) -> p a b", a=2), ACT.Square,
                                       accum_out=stat[:, 0, i:i + 1]))
                act.wait_ge(S["pads"], 1)
                step(sc.activation(stat[:, 0, :], stat[:, 0, :], ACT.Sqrt, bias=eps_col, scale=1.0 / D), "ssq_ready")

            def norm_out(n):
                for i in range(T):
                    if n == 1:
                        act.wait_ge(S["h_ready"], T + i + 1)
                        act.dma_start(t["h_scratch"][i * P:(i + 1) * P, :], h2_tok[:, i % 2, :]).then_inc(S[f"h2_out{i % 2}"], 16)
                    for g in range(2):
                        act.wait_ge(S["hT_mm"], 2 * (n * T + i) + g + 1)
                        step(sc.activation(hT[:, 4 * g:4 * g + 4, tok0[i]:tok0[i] + P],
                                           banks[4 + g][:, :].rearrange("p (a b) -> p a b", a=4), ACT.Copy), "hT_ready")

            norm_act(0, x_sb)
            for j in range(4):
                bc_copy(j)
            norm_out(0)
            act.wait_ge(S["kctxT_mm"], 1)
            step(sc.activation(kctxT, banks[6][:, :].rearrange("p (a b) -> p a b", a=4), ACT.Copy), "kctxT_ready")
            for u in range(2 * T):
                act.wait_ge(S["proj_mm"], u + 1)
                if u >= 2:
                    act.wait_ge(S["headsum"], u - 1)
                step(sc.activation(square[:, u % 2, :], banks[u % 4][:, :], ACT.Square), "squared")
                act.wait_ge(S["headsum"], u + 1)
                step(sc.activation(headstat[:, u % 2, 8:16], headstat[:, u % 2, 0:8], ACT.Sqrt, bias=eps_col,
                                   scale=1.0 / D_HA), "headstd")
                if u >= 1:
                    v = u - 1
                    act.wait_ge(S["qkT_mm"], v + 1)
                    src = banks[4 + v % 2][:, :].rearrange("p (a b) -> p a b", a=4)
                    if 1 <= v < T:
                        for r in range(2):
                            step(sc.activation(qa_blocks[:, :, :, 2 * (v - 1) + r, :],
                                               src[:, :, r * GRID_W:(r + 1) * GRID_W].rearrange("p a (m c) -> p a m c", m=N_CB),
                                               ACT.Copy), "qkT_ready" if r else "act_step")
                    else:
                        step(sc.activation((qaT if v < T else kaT)[:, :, tok0[v % T]:tok0[v % T] + P], src, ACT.Copy), "qkT_ready")
            v = 2 * T - 1
            act.wait_ge(S["qkT_mm"], v + 1)
            step(sc.activation(kaT[:, :, tok0[T - 1]:tok0[T - 1] + P],
                               banks[4 + v % 2][:, :].rearrange("p (a b) -> p a b", a=4), ACT.Copy), "qkT_ready")
            for i in range(T):
                u = 2 * T + i
                act.wait_ge(S["proj_mm"], u + 1)
                if i >= 3:
                    act.wait_ge(S[f"v_scratch{i % 2}"], 16)
                dst = va0 if i == 0 else va_out[:, i % 2, :]
                step(sc.activation(dst, banks[u % 4][:, :], ACT.Copy), "va_ready")

            NU = 8 * (1 + N_CB)

            def probs_out(u):
                w = P if u < 8 else KEYS
                act.wait_ge(S["probT_mm"], u + 1)
                if u >= 2:
                    act.wait_ge(S["pv_mm"], u - 1)
                step(sc.activation(probT[:, u % 2, 0:w], banks[2 + u % 2][:, 0:w], ACT.Copy), "probT_ready")

            for u in range(NU):
                w = P if u < 8 else KEYS
                act.wait_ge(S["max_ready"], u + 1)
                step(sc.activation(score[:, u % 2, 0:w], score[:, u % 2, 0:w], ACT.Exp, bias=sstat[:, u % 2, 0:1],
                                   accum_out=sstat[:, u % 2, 1:2]), "exp_done")
                if u >= 1:
                    probs_out(u - 1)
            probs_out(NU - 1)
            barrier(act, 1)

            act.wait_ge(S["g_raw"], 1)
            step(sc.activation(gt[:, 6:8, :], gt[:, 1:3, :], ACT.Exp, scale=-1.0))
            step(sc.activation(gt[:, 8, 0:8], rows[:, R_AL:R_AL + 8], ACT.Exp))
            step(sc.activation(gt[:, 6, :], gt[:, 6, :], ACT.Ln, bias=ones[:, 0:1]), "g_act")
            act.wait_ge(S["gc_used"], 1)
            step(sc.activation(gt[:, 4:6, :], gt[:, 10:12, :], ACT.Exp))
            step(sc.activation(gt[:, 9, :], gt[:, 9, :], ACT.Exp), "gexp_done")

            def silu_out(c):
                act.wait_ge(S["conv_ready"], c + 1)
                if c >= 2:
                    act.wait_ge(S["tok_mm"], c - 1)
                step(sc.activation(ys[:, c % 2, :], yc[:, c % 2, :], ACT.Silu), "ys_ready")

            for c in range(12):
                act.wait_ge(S["cm_mm"], c + 1)
                if c >= 2:
                    act.wait_ge(S["conv_ready"], c - 1)
                else:
                    act.wait_ge(S["pads"], 2)
                step(sc.activation(xc[:, c % 2, 2:2 + SEQ], banks[2 * (c % 2) + 1][:, 0:SEQ], ACT.Copy))
                step(sc.activation(xc[:, c % 2, 4 + SEQ:4 + TOK], banks[2 * (c % 2)][:, :], ACT.Copy), "xc_ready")
                if c >= 1:
                    silu_out(c - 1)
            silu_out(11)
            for i in range(T):
                if i == 0:
                    act.wait_ge(S["tok_ready"], 12)
                if i >= 2:
                    act.wait_ge(S["qksum"], i - 1)
                step(sc.activation(sq_b[:, i % 2, :], qkv[:, i, 0:2 * W_B], ACT.Square), "sq_ready")
            act.wait_ge(S["qksum"], T)
            step(sc.activation(qkstat[:, :, 8:16], qkstat[:, :, 0:8], ACT.Sqrt, bias=eps_col), "qkstd")
            for i in range(T):
                for g in range(2):
                    act.wait_ge(S["kqT_mm"], 2 * i + g + 1)
                    step(sc.activation((qdT, kdT)[g][:, :, tok0[i]:tok0[i] + P],
                                       banks[2 * (i % 2) + g][:, :].rearrange("p (a b) -> p a b", a=4), ACT.Copy), "kqT_ready")
            
            for p in range(T):
                for d in range(2):
                    U = unit[d]
                    B0 = banks[4 * d][:, :].rearrange("p (h c) -> p h c", h=H_B)
                    act.wait_ge(S[f"row_mm{d}"], p + 1)
                    if p >= 1:
                        act.wait_ge(S[f"o_mm{d}"], 2 * p)
                    step(sc.activation(U["erow"], B0, ACT.Exp), f"erow{d}")
                    act.wait_ge(S[f"dpre{d}"], p + 1)
                    step(sc.activation(U["decayT"], U["decayT"], ACT.Exp), f"dexp{d}")
                for n in range(len(LEVELS)):
                    for d in range(2):
                        U = unit[d]
                        B0 = banks[4 * d][:, :].rearrange("p (h c) -> p h c", h=H_B)
                        act.wait_ge(S[f"x_mm{d}"], len(LEVELS) * p + n + 1)
                        if n >= 1:
                            act.wait_ge(S[f"p_mm{d}"], len(LEVELS) * p + n)
                        step(sc.activation(U["xs"], B0, ACT.Copy), f"xs{d}")
                for d in range(2):
                    U = unit[d]
                    B0 = banks[4 * d][:, :].rearrange("p (h c) -> p h c", h=H_B)
                    act.wait_ge(S[f"wt_mm{d}"], p + 1)
                    step(sc.activation(U["nwT"], B0, ACT.Copy, scale=-1.0), f"nwt{d}")
            barrier(act, 2)

            for i in range(T):
                if i >= 2:
                    act.wait_ge(S["osum"], i - 1)
                step(sc.activation(osq[:, i % 2, :], o_acc[:, i, :], ACT.Square), "osq_ready")
            act.wait_ge(S["osum"], T)
            step(sc.activation(ostat[:, :, 4:8], ostat[:, :, 0:4], ACT.Sqrt, bias=eps_col, scale=1.0 / DK), "ostd")

            def ob_out(i):
                act.wait_ge(S["obT_mm"], i + 1)
                step(sc.activation(obT[:, :, tok0[i]:tok0[i] + P],
                                   banks[4 + i % 2][:, :].rearrange("p (a b) -> p a b", a=4), ACT.Copy), "obT_ready")

            for i in range(T):
                act.wait_ge(S["z_mm"], i + 1)
                if i >= 2:
                    act.wait_ge(S["ob_ready"], i - 1)
                step(sc.activation(zs[:, i % 2, :], banks[i % 2][:, :], ACT.Silu), "zs_ready")
                if i >= 1:
                    ob_out(i - 1)
            ob_out(T - 1)
            for j in range(4, 12):
                bc_copy(j)
            for u in range(NHALF * T):
                b = 4 * (u % 2)
                act.wait_ge(S["merge_mm"], u + 1)
                if u >= 2:
                    act.wait_ge(S["merged_ready"], u - 1)
                step(sc.activation(sga[:, u % 2, :], banks[b + 2][:, :], ACT.Sigmoid))
                step(sc.activation(sgb[:, u % 2, :], banks[b + 3][:, :], ACT.Sigmoid), "sig_ready")
            for i in range(T):
                for g in range(2):
                    act.wait_ge(S["mT_mm"], 2 * i + g + 1)
                    step(sc.activation(hT[:, 4 * g:4 * g + 4, tok0[i]:tok0[i] + P],
                                       banks[4 + g][:, :].rearrange("p (a b) -> p a b", a=4), ACT.Copy), "mT_ready")
            act.wait_ge(S["out_mm"], T * NHALF)
            norm_act(1, x2)
            norm_out(1)
            act.wait_ge(S["router_exp_in"], 1)
            step(sc.activation(ex[:, 1], ex[:, 0], ACT.Exp), "router_exp")
            barrier(act, 3)

            act.wait_ge(S["dense_ready"], 1)
            is_dense = act.value_load(dense[0:1, 0:1])
            with act.If(is_dense > 0):
                step = stepper(act, "act_step", dict(steps))
                def hid_out(u):
                    act.wait_ge(S["hidT_mm"], u + 1)
                    if u >= 2:
                        act.wait_ge(S["down_mm"], u - 1)
                    step(sc.activation(hidT[:, u % 2, 0:2 * P], banks[2 + u % 2][:, 0:2 * P], ACT.Copy), "hidT_ready")

                for u in range(N_EXPERTS * T):
                    act.wait_ge(S["eup_mm"], u + 1)
                    if u >= 2:
                        act.wait_ge(S["hid_ready"], u - 1)
                    step(sc.activation(sg[:, u % 2, 0:D_FF], banks[u % 2][:, 0:D_FF], ACT.Silu), "silu_done")
                    if u >= 1:
                        hid_out(u - 1)
                hid_out(N_EXPERTS * T - 1)
            with act.Else():
                step = stepper(act, "act_step", dict(steps))

                def rowsT_out(e):
                    act.wait_ge(S["rowsT_mm"], 2 * e + 1)
                    if e >= 2:
                        act.wait_ge(S["eup_mm"], e - 1)
                    step(sc.activation(rowsT[e % 2][:, 0:4, :], banks[0][:, :].rearrange("p (k n) -> p k n", k=4), ACT.Copy), "rowsT_ready")

                def out_rows(e):
                    act.wait_ge(S["down_mm"], e + 1)
                    if e >= 3:
                        act.wait_ge(S[f"expert_out{e % 3}"], 16 * (e // 3))
                    step(sc.activation(rows_out[e % 3][:, 0:HALF], banks[6][:, :], ACT.Copy), "acc_done")

                rowsT_out(0)
                for e in range(N_EXPERTS):
                    act.wait_ge(S["eup_mm"], e + 1)
                    if e >= 2:
                        act.wait_ge(S["hid_ready"], e - 1)
                    step(sc.activation(sg[:, e % 2, 0:D_FF], banks[2 + e % 2][:, 0:D_FF], ACT.Silu), "silu_done")
                    if e + 1 < N_EXPERTS:
                        rowsT_out(e + 1)
                    if e >= 1:
                        out_rows(e - 1)
                    act.wait_ge(S["hidT_mm"], e + 1)
                    step(sc.activation(hidT[:, e % 2, 0:2 * P], banks[4 + e % 2][:, 0:2 * P], ACT.Copy), "hidT_ready")
                out_rows(N_EXPERTS - 1)
                for i in range(T):
                    act.wait_ge(S[f"w_in{i % 2}"], expert_loaded(N_EXPERTS - 2 + i % 2) + 32 * (i // 2 + 1))
                    a = rows_in[2 * (i % 2)]
                    step(sc.activation(a, a, ACT.Copy, scale=wts[:, 1, i, :]), "weighted")

        @block.vector
        def _(dve):
            steps = {}
            step = stepper(dve, "dve_step", steps)
            v = nc.vector
            step(v.memset(eps_col, EPS), "pads")
            dve.wait_ge(S["consts_in"], 64)

            def mod_rows(j):
                dve.wait_ge(S["mod_mm"], j + 1)
                if j >= 2:
                    dve.wait_ge(S["bc_mm"], 2 * (j - 1))
                r = mod_row[0:2, j % 2, :]
                kind, half = j // 2, j % 2
                b = bmod_a[0:2, j, :] if j < 4 else bmod_c[0:2, j - 4, :]
                if kind in (1, 4):
                    step(v.tensor_tensor(r, banks[j % 2][0:2, :], b, ALU.add))
                    step(v.scalar_tensor_tensor(r, r, 1.0, (norm_a, norm_c)[kind // 3][0:2, half * HALF:(half + 1) * HALF],
                                                ALU.add, ALU.mult), "row_ready")
                else:
                    step(v.tensor_tensor(r, banks[j % 2][0:2, :], b, ALU.add), "row_ready")

            def norm_dve(n, x, h):
                dve.wait_ge(S["ssq_ready"], n + 1)
                step(v.reciprocal(stat[:, 1, :], stat[:, 0, :]))
                dve.wait_ge(S["bc_done"], (8, 24)[n])
                for i in range(T):
                    c = min(i, 1)
                    if i >= 2:
                        dve.wait_ge(S["hT_mm"], 2 * (n * T + i - 1))
                    if n == 1 and i >= 2:
                        dve.wait_ge(S[f"h2_out{i % 2}"], 16 * (i // 2))
                    step(v.scalar_tensor_tensor(h[:, i % 2, :], x[:, i, :], stat[:, 1, i:i + 1], scale_bc[:, c, :], ALU.mult, ALU.mult))
                    step(v.tensor_tensor(h[:, i % 2, :], h[:, i % 2, :], shift_bc[:, c, :], ALU.add), "h_ready")

            for j in range(4):
                mod_rows(j)
            norm_dve(0, x_sb, h_tok)
            dve.wait_ge(S["hT_mm"], 2 * T)
            for u in range(2 * T):
                hs = headstat[:, u % 2, :]
                dve.wait_ge(S["squared"], u + 1)
                step(v.tensor_reduce(hs[:, 0:8], square[:, u % 2, :].rearrange("p (h c) -> p h c", h=H_A), AX_X, ALU.add), "headsum")
                dve.wait_ge(S["headstd"], u + 1)
                step(v.reciprocal(hs[:, 16:24], hs[:, 8:16]))
                if u >= 2:
                    dve.wait_ge(S["qkT_mm"], u - 1)
                if u == T + 2:
                    dve.wait_ge(S["k_out"], 16)
                q = qk_tok[:, u % 2, :].rearrange("p (h c) -> p h c", h=H_A)
                step(v.tensor_tensor(q, banks[u % 4][:, :].rearrange("p (h c) -> p h c", h=H_A),
                                     hs[:, 16:24].unsqueeze(2).to_broadcast([P, H_A, D_HA]), ALU.mult))
                w = rows[:, R_QN:R_QN + 64] if u < T else rows[:, R_KN:R_KN + 64]
                step(v.tensor_tensor(q, q, w.unsqueeze(1).to_broadcast([P, H_A, D_HA]), ALU.mult), "qk_ready")

            NU = 8 * (1 + N_CB)

            def pv_out(u):
                pair = u // 2
                dve.wait_ge(S["pv_mm"], 2 * pair + 2)
                b = banks[4 + pair % 2]
                h2 = pair % 4
                if u < 8:
                    dst, src = oaT[:, h2, 0:SEQ], b[:, 0:P]
                else:
                    m = u // 8 - 1
                    dst = oaT[:, h2, SEQ:TOK].rearrange("p (r c) -> p r c", c=GRID_W)[:, :, m * QB_W:(m + 1) * QB_W]
                    src = b[:, 0:P].rearrange("p (r c) -> p r c", c=QB_W)
                step(v.tensor_copy(dst, src), "pv_used")

            for u in range(NU):
                w = P if u < 8 else KEYS
                s = score[:, u % 2, 0:w]
                dve.wait_ge(S["score_mm"], u + 1)
                if u >= 2:
                    dve.wait_ge(S["probT_mm"], u - 1)
                if u < 8:
                    step(v.tensor_scalar(s, banks[u % 2][:, 0:w], D_HA ** -0.5, None, ALU.mult))
                else:
                    m, h = u // 8 - 1, u % 8
                    if h == 0:
                        dve.wait_ge(S[f"bias_in{BIAS_OF[m] % 2}"], 16 * (BIAS_OF[m] // 2 + 1))
                    step(v.scalar_tensor_tensor(s, banks[u % 2][:, 0:w], D_HA ** -0.5, bias[:, BIAS_OF[m] % 2, h, :], ALU.mult, ALU.add))
                step(v.tensor_reduce(sstat[:, u % 2, 0:1], s, AX_X, ALU.max, negate=True), "max_ready")
                dve.wait_ge(S["exp_done"], u + 1)
                step(v.reciprocal(sstat[:, u % 2, 2:3], sstat[:, u % 2, 1:2]))
                step(v.tensor_scalar(s, s, sstat[:, u % 2, 2:3], None, ALU.mult), "prob_ready")
                if u >= 3 and u % 2 == 1:
                    pv_out(u - 2)
            pv_out(NU - 1)
            barrier(dve, 1)

            step(v.memset(xc, 0.0), "pads")
            dve.wait_ge(S["b_in"], 64)
            dve.wait_ge(S["ab_mm"], 1)
            step(v.tensor_copy(ab, banks[7][:, 0:T * 16].rearrange("p (a b) -> p a b", a=T)))
            a_by_dir = ab[:, :, 0:8].rearrange("p t (d h) -> p d t h", d=2)
            b_by_dir = ab[:, :, 8:16].rearrange("p t (d h) -> p d t h", d=2)
            for d in range(2):
                g0 = gt[:, 0, d * T * H_B:(d + 1) * T * H_B].rearrange("p (t h) -> p t h", t=T)
                step(v.tensor_tensor(g0, a_by_dir[:, d], rows[:, R_DT + 4 * d:R_DT + 4 * d + 4].unsqueeze(1).to_broadcast([P, T, H_B]), ALU.add))
                step(v.tensor_copy(gt[:, 2, d * T * H_B:(d + 1) * T * H_B].rearrange("p (t h) -> p t h", t=T), b_by_dir[:, d]))
            step(v.scalar_tensor_tensor(gt[:, 1, :], gt[:, 0, :], -1.0, gt[:, 0, :], ALU.mult, ALU.max), "g_raw")
            dve.wait_ge(S["g_act"], 1)
            step(v.scalar_tensor_tensor(gt[:, 6, :], gt[:, 0, :], 0.0, gt[:, 6, :], ALU.max, ALU.add))
            for d in range(2):
                gd = gt[:, 0, d * T * H_B:(d + 1) * T * H_B].rearrange("p (t h) -> p t h", t=T)
                sd = gt[:, 6, d * T * H_B:(d + 1) * T * H_B].rearrange("p (t h) -> p t h", t=T)
                step(v.scalar_tensor_tensor(gd, sd, -1.0, gt[:, 8, 4 * d:4 * d + 4].unsqueeze(1).to_broadcast([P, T, H_B]), ALU.mult, ALU.mult))
            step(v.tensor_scalar(gt[:, 7, :], gt[:, 7, :], 1.0, None, ALU.add))
            step(v.reciprocal(gt[:, 3, :], gt[:, 7, :]), "g_ready")
            dve.wait_ge(S["gc_mm"], 1)
            n = 2 * T * H_B
            step(v.tensor_copy(gt[:, 9:11, :], banks[7][:, 128:128 + 2 * n].rearrange("p (a b) -> p a b", a=2)))
            step(v.tensor_tensor(gt[:, 11, :], gt[:, 9, :], gt[:, 10, :], ALU.subtract), "gc_used")

            def tok_out(c):
                dve.wait_ge(S["tok_mm"], c + 1)
                b = 4 + 2 * (c % 2)
                step(v.tensor_copy(qkv[:, 0, c * P:(c + 1) * P], banks[b + 1][:, 0:P]))
                step(v.tensor_copy(qkv[:, 1:T, c * P:(c + 1) * P], banks[b][:, :].rearrange("p (a b) -> p a b", a=4)), "tok_ready")

            for c in range(12):
                dve.wait_ge(S["xc_ready"], c + 1)
                if c >= 2:
                    dve.wait_ge(S["ys_ready"], c - 1)
                y = yc[:, c % 2, :]
                step(v.tensor_scalar(y, xc[:, c % 2, 0:YC], conv_w[:, c, 0:1], None, ALU.mult))
                for j in range(1, CONV_K):
                    step(v.scalar_tensor_tensor(y, xc[:, c % 2, j:j + YC], conv_w[:, c, j:j + 1], y, ALU.mult, ALU.add),
                         "conv_ready" if j == CONV_K - 1 else "dve_step")
                if c >= 1:
                    tok_out(c - 1)
            tok_out(11)
            for i in range(T):
                dve.wait_ge(S["sq_ready"], i + 1)
                step(v.tensor_reduce(qkstat[:, i, 0:8], sq_b[:, i % 2, :].rearrange("p (h c) -> p h c", h=8), AX_X, ALU.add), "qksum")
            dve.wait_ge(S["qkstd"], 1)
            step(v.reciprocal(qkstat[:, :, 0:8], qkstat[:, :, 8:16]))
            step(v.tensor_scalar(qkstat[:, :, 0:4], qkstat[:, :, 0:4], DK ** -0.5, None, ALU.mult))
            for i in range(T):
                qk = qkv[:, i, 0:2 * W_B].rearrange("p (h c) -> p h c", h=8)
                step(v.tensor_tensor(qk, qk, qkstat[:, i, 0:8].unsqueeze(2).to_broadcast([P, 8, DK]), ALU.mult),
                     "rope_done" if i == 0 else "dve_step")
                if i >= 1:
                    pairs = qkv[:, i, 0:2 * W_B].rearrange("p (h c two) -> p h c two", h=8, two=2)
                    x1, x2_ = pairs[:, :, :, 0], pairs[:, :, :, 1]
                    cos = rope[:, i - 1, 0, :].unsqueeze(1).to_broadcast([P, 8, 64])
                    sin = rope[:, i - 1, 1, :].unsqueeze(1).to_broadcast([P, 8, 64])
                    step(v.tensor_tensor(ropet[:, 0], x1, cos, ALU.mult))
                    step(v.tensor_tensor(ropet[:, 1], x2_, sin, ALU.mult))
                    step(v.tensor_tensor(ropet[:, 2], x1, sin, ALU.mult))
                    step(v.tensor_tensor(ropet[:, 3], x2_, cos, ALU.mult))
                    step(v.tensor_tensor(x1, ropet[:, 0], ropet[:, 1], ALU.subtract))
                    step(v.tensor_tensor(x2_, ropet[:, 2], ropet[:, 3], ALU.add), "rope_done")
            dve.wait_ge(S["kqT_ready"], 2 * T)
            dve.wait_ge(S["gexp_done"], 1)
            for d in range(2):
                step(v.memset(unit[d]["state"], 0.0), f"st{d}")
            for p in range(T):
                for d in range(2):
                    U = unit[d]
                    i = 0 if p == 0 else (p if d == 0 else T - p)
                    col = (d * T + i) * H_B
                    A = banks[4 * d][:, :].rearrange("p (h c) -> p h c", h=H_B)
                    B = banks[4 * d + 1][:, :].rearrange("p (h c) -> p h c", h=H_B)
                    C = banks[4 * d + 2][:, :].rearrange("p (h c) -> p h c", h=H_B)
                    dve.wait_ge(S[f"row_mm{d}"], p + 1)
                    dve.wait_ge(S[f"erow{d}"], p + 1)
                    for h in range(H_B):
                        step(v.scalar_tensor_tensor(U["decayT"][:, h], A[:, h], gt[:, 10, col + h:col + h + 1], negmask[d],
                                                    ALU.subtract, ALU.add), f"dpre{d}" if h == H_B - 1 else "dve_step")
                    dve.wait_ge(S[f"dexp{d}"], p + 1)
                    dve.wait_ge(S[f"kq_mm{d}"], p + 1)
                    if p >= 1:
                        dve.wait_ge(S[f"o_mm{d}"], 2 * p)
                    step(v.tensor_tensor(U["gramT"], B, U["decayT"], ALU.mult), f"bt{d}")
                    step(v.tensor_tensor(U["intraT"], C, U["decayT"], ALU.mult), f"bt{d}")
                for n in range(len(LEVELS)):
                    for d in range(2):
                        U = unit[d]
                        B = banks[4 * d + 1][:, :].rearrange("p (h c) -> p h c", h=H_B)
                        C = banks[4 * d + 2][:, :].rearrange("p (h c) -> p h c", h=H_B)
                        dve.wait_ge(S[f"p_mm{d}"], len(LEVELS) * p + n + 1)
                        step(v.tensor_tensor(U["inv"], U["inv"], B, ALU.subtract))
                        step(v.tensor_tensor(U["invT"], U["invT"], C, ALU.subtract), f"mn{d}")
                for d in range(2):
                    U = unit[d]
                    B = banks[4 * d + 1][:, :].rearrange("p (h c) -> p h c", h=H_B)
                    dve.wait_ge(S[f"vn_mm{d}"], p + 1)
                    step(v.tensor_copy(U["vnew"], B), f"vn{d}")
                for d in range(2):
                    U = unit[d]
                    i = 0 if p == 0 else (p if d == 0 else T - p)
                    col = (d * T + i) * H_B
                    C = banks[4 * d + 2][:, :].rearrange("p (h c) -> p h c", h=H_B)
                    O = banks[4 * d + 3][:, :]
                    first = d == 0 if p == 0 else p <= 2
                    dve.wait_ge(S[f"o_mm{d}"], 2 * p + 1)
                    if first:
                        step(v.tensor_copy(o_acc[:, i, :], O), f"os{d}")
                    else:
                        step(v.tensor_tensor(o_acc[:, i, :], o_acc[:, i, :], O, ALU.add), f"os{d}")
                    dve.wait_ge(S[f"o_mm{d}"], 2 * p + 2)
                    for h in range(H_B):
                        step(v.scalar_tensor_tensor(U["state"][:, h], U["state"][:, h], gt[:, 9, col + h:col + h + 1], C[:, h],
                                                    ALU.mult, ALU.add), f"os{d}" if h == H_B - 1 else "dve_step")
                if p == 0:
                    dve.wait_ge(S["states_in"], 64)
            barrier(dve, 2)

            for i in range(T):
                dve.wait_ge(S["osq_ready"], i + 1)
                step(v.tensor_reduce(ostat[:, i, 0:4], osq[:, i % 2, :].rearrange("p (h c) -> p h c", h=4), AX_X, ALU.add), "osum")
            dve.wait_ge(S["ostd"], 1)
            step(v.reciprocal(ostat[:, :, 0:4], ostat[:, :, 4:8]))
            onw = rows[:, R_ON:R_ON + DK].unsqueeze(1).to_broadcast([P, H_B, DK])
            for i in range(T):
                o = o_acc[:, i, :].rearrange("p (h c) -> p h c", h=4)
                step(v.tensor_tensor(o, o,
                                     ostat[:, i, 0:4].unsqueeze(2).to_broadcast([P, H_B, DK]), ALU.mult))
                step(v.tensor_tensor(o, o, onw, ALU.mult))
                dve.wait_ge(S["zs_ready"], i + 1)
                step(v.tensor_tensor(o_acc[:, i, :], o_acc[:, i, :], zs[:, i % 2, :], ALU.mult), "ob_ready")
            dve.wait_ge(S["b_in"], 112)
            for j in range(4, 12):
                mod_rows(j)
            for u in range(NHALF * T):
                n, i = u // T, u % T
                b = 4 * (u % 2)
                dve.wait_ge(S["sig_ready"], u + 1)
                step(v.tensor_tensor(sga[:, u % 2, :], sga[:, u % 2, :], banks[b][:, :], ALU.mult))
                step(v.tensor_tensor(sgb[:, u % 2, :], sgb[:, u % 2, :], banks[b + 1][:, :], ALU.mult))
                step(v.tensor_tensor(merged[:, i, n * HALF:(n + 1) * HALF], sga[:, u % 2, :], sgb[:, u % 2, :], ALU.add), "merged_ready")
            for i in range(T):
                dve.wait_ge(S[f"x_in{i}"], 32)
            for u in range(NHALF * T):
                n, i = u // T, u % T
                c = min(i, 1)
                cols = slice(n * HALF, (n + 1) * HALF)
                dve.wait_ge(S["out_mm"], u + 1)
                step(v.tensor_tensor(sga[:, u % 2, :], gate1_bc[:, c, cols], banks[u % 4][:, :], ALU.mult))
                step(v.tensor_tensor(x2[:, i, cols], x2[:, i, cols], sga[:, u % 2, :], ALU.add), "x2_ready")
            norm_dve(1, x2, h2_tok)
            first4 = rows[:, R_FIRST + 4:R_FIRST + 8].unsqueeze(1).to_broadcast([P, T, 4])
            first8 = rows[:, R_FIRST:R_FIRST + 8].unsqueeze(1).to_broadcast([P, T, 8])
            dve.wait_ge(S["logit_mm"], 1)
            step(v.tensor_tensor(logit, banks[0][:, 0:T * 36].rearrange("p (t n) -> p t n", t=T),
                                 rows[:, R_BR:R_BR + 36].unsqueeze(1).to_broadcast([P, T, 36]), ALU.add))
            groups = logit[:, :, 0:N_GROUPS]
            step(v.tensor_reduce(gmax, groups, AX_X, ALU.max))
            step(v.tensor_tensor(ex[:, 0, :, 0:4], groups, gmax.to_broadcast([P, T, 4]), ALU.subtract))
            step(v.tensor_tensor(geq, groups, gmax.to_broadcast([P, T, 4]), ALU.is_equal))
            step(v.tensor_tensor(geq, geq, first4, ALU.mult))
            step(v.tensor_reduce(gmax, geq, AX_X, ALU.max))
            step(v.tensor_tensor(gsel, geq, gmax.to_broadcast([P, T, 4]), ALU.is_equal))
            step(v.tensor_tensor(eprod, logit[:, :, N_GROUPS:].rearrange("p t (g e) -> p t g e", g=N_GROUPS),
                                 gsel.unsqueeze(3).to_broadcast([P, T, 4, 8]), ALU.mult))
            step(v.tensor_reduce(ingrp, eprod.rearrange("p t g e -> p t e g"), AX_X, ALU.add))
            for r in range(2):
                step(v.tensor_reduce(emax[:, r], ingrp, AX_X, ALU.max))
                step(v.tensor_tensor(eeq, ingrp, emax[:, r].to_broadcast([P, T, 8]), ALU.is_equal))
                step(v.tensor_tensor(eeq, eeq, first8, ALU.mult))
                step(v.tensor_reduce(emax[:, 2], eeq, AX_X, ALU.max))
                step(v.tensor_tensor(esel[:, r], eeq, emax[:, 2].to_broadcast([P, T, 8]), ALU.is_equal))
                if r == 0:
                    step(v.scalar_tensor_tensor(ingrp, esel[:, 0], -BIG, ingrp, ALU.mult, ALU.add))
            step(v.tensor_tensor(ex[:, 0, :, 4:5], emax[:, 1], emax[:, 0], ALU.subtract), "router_exp_in")
            dve.wait_ge(S["router_exp"], 1)
            step(v.tensor_reduce(wts[:, 0], ex[:, 1, :, 0:4], AX_X, ALU.add))
            step(v.scalar_tensor_tensor(wts[:, 0], ex[:, 1, :, 4:5], 1.0, wts[:, 0], ALU.add, ALU.mult))
            step(v.reciprocal(wts[:, 1], wts[:, 0]))
            step(v.tensor_tensor(wts[:, 2], wts[:, 1], ex[:, 1, :, 4:5], ALU.mult))
            for r in range(2):
                step(v.tensor_tensor(chosen[:, r].rearrange("p t (g e) -> p t g e", g=N_GROUPS), esel[:, r].unsqueeze(2).to_broadcast([P, T, 4, 8]),
                                     gsel.unsqueeze(3).to_broadcast([P, T, 4, 8]), ALU.mult))
            step(v.tensor_tensor(picked, chosen[:, 0], chosen[:, 1], ALU.add), "chosen_ready")
            for r in range(2):
                step(v.tensor_tensor(esel[:, r], esel[:, r], wts[:, 1 + r].to_broadcast([P, T, 8]), ALU.mult))
            step(v.tensor_tensor(eeq, esel[:, 0], esel[:, 1], ALU.add))
            step(v.tensor_tensor(combine.rearrange("p t (g e) -> p t g e", g=N_GROUPS), eeq.unsqueeze(2).to_broadcast([P, T, 4, 8]),
                                 gsel.unsqueeze(3).to_broadcast([P, T, 4, 8]), ALU.mult))
            dve.wait_ge(S["place_mm"], 1)
            step(v.tensor_reduce(most, banks[1][:, T * N_EXPERTS:(T + 1) * N_EXPERTS], AX_X, ALU.max))
            step(v.tensor_scalar(most, most, float(CAP), None, ALU.is_gt))
            step(v.tensor_copy(dense, most), "dense_ready")
            step(v.scalar_tensor_tensor(place, banks[1][:, 0:T * N_EXPERTS].rearrange("p (t e) -> p t e", t=T), float(N_EXPERTS),
                                        rows[:, R_IOTA:R_IOTA + N_EXPERTS].unsqueeze(1).to_broadcast([P, T, N_EXPERTS]), ALU.mult, ALU.add))
            for r in range(2):
                step(v.tensor_tensor(chosen[:, r], chosen[:, r], place, ALU.mult))
                step(v.tensor_reduce(dest[:, r, :].unsqueeze(2), chosen[:, r], AX_X, ALU.add))
            step(v.tensor_copy(dest_i, dest), "dest_ready")
            barrier(dve, 3)

            is_dense = dve.value_load(dense[0:1, 0:1])
            with dve.If(is_dense > 0):
                step = stepper(dve, "dve_step", dict(steps))
                step(v.memset(acc, 0.0))

                def acc_add(u):
                    dve.wait_ge(S["down_mm"], u + 1)
                    for n in range(NHALF):
                        part = acc[:, u % T, n * HALF:(n + 1) * HALF]
                        step(v.tensor_tensor(part, part, banks[4 + 2 * (u % 2) + n][:, :], ALU.add), "acc_done" if n else "dve_step")

                for u in range(N_EXPERTS * T):
                    e, i = u // T, u % T
                    dve.wait_ge(S["silu_done"], u + 1)
                    if u >= 2:
                        dve.wait_ge(S["hidT_mm"], u - 1)
                    step(v.scalar_tensor_tensor(hid[:, u % 2, 0:D_FF], sg[:, u % 2, 0:D_FF], combine[:, i, e:e + 1],
                                                banks[u % 2][:, D_FF:2 * D_FF], ALU.mult, ALU.mult), "hid_ready")
                    if u >= 1:
                        acc_add(u - 1)
                acc_add(N_EXPERTS * T - 1)
                for i in range(T):
                    c = min(i, 1)
                    step(v.tensor_tensor(acc[:, i, :], acc[:, i, :], gate2_bc[:, c, :], ALU.mult))
                    step(v.tensor_tensor(x2[:, i, :], x2[:, i, :], acc[:, i, :], ALU.add), "y_ready")
            with dve.Else():
                step = stepper(dve, "dve_step", dict(steps))
                step(v.memset(shift_bc, 0.0))
                step(v.memset(scale_bc, 0.0), "rows_clear")

                def rowsT_out(e):
                    dve.wait_ge(S["rowsT_mm"], 2 * e + 2)
                    if e >= 2:
                        dve.wait_ge(S["eup_mm"], e - 1)
                    step(v.tensor_copy(rowsT[e % 2][:, 4:8, :], banks[1][:, :].rearrange("p (k n) -> p k n", k=4)), "rowsT_ready2")

                def out_rows(e):
                    dve.wait_ge(S["down_mm"], e + 1)
                    if e >= 3:
                        dve.wait_ge(S[f"expert_out{e % 3}"], 16 * (e // 3))
                    step(v.tensor_copy(rows_out[e % 3][:, HALF:D], banks[7][:, :]), "s_out2")

                rowsT_out(0)
                for e in range(N_EXPERTS):
                    dve.wait_ge(S["silu_done"], e + 1)
                    if e >= 2:
                        dve.wait_ge(S["hidT_mm"], e - 1)
                    step(v.tensor_tensor(hid[:, e % 2, 0:D_FF], sg[:, e % 2, 0:D_FF], banks[2 + e % 2][:, D_FF:2 * D_FF], ALU.mult), "hid_ready")
                    if e + 1 < N_EXPERTS:
                        rowsT_out(e + 1)
                    if e >= 1:
                        out_rows(e - 1)
                out_rows(N_EXPERTS - 1)
                for i in range(T):
                    c = min(i, 1)
                    a, b = rows_in[2 * (i % 2)], rows_in[2 * (i % 2) + 1]
                    dve.wait_ge(S["weighted"], i + 1)
                    step(v.scalar_tensor_tensor(a, b, wts[:, 2, i, :], a, ALU.mult, ALU.add))
                    step(v.tensor_tensor(a, a, gate2_bc[:, c, :], ALU.mult))
                    step(v.tensor_tensor(x2[:, i, :], x2[:, i, :], a, ALU.add), "y_ready")

        @block.tensor
        def _(pe):
            mm = nc.tensor.matmul

            def mod_mm(j):
                w = ringv[:, w_slot(f"mod{j}")]
                if j == 0:
                    pe.wait_ge(S["silu_c"], 1)
                w_wait(pe, f"mod{j}")
                if j >= 2:
                    pe.wait_ge(S["row_ready"], j - 1)
                for k in range(KC):
                    last = mm(banks[j % 2][0:2, :], silu_cT[:, k, :], w[:, k, :], start=(k == 0), stop=(k == KC - 1))
                last.then_inc(S["mod_mm"], 1)

            def mod_bc(j):
                pe.wait_ge(S["row_ready"], j + 1)
                pe.wait_ge(S["consts_in"], 64)
                for c in range(2):
                    if j >= 1:
                        pe.wait_ge(S["bc_done"], 2 * (j - 1) + c + 1)
                    last = mm(banks[2 + c][:, :], pick[c], mod_row[0:2, j % 2, :], start=True, stop=True)
                    last.then_inc(S["bc_mm"], 1)

            def turns(n, h):
                for i in range(T):
                    pe.wait_ge(S["h_ready"], n * T + i + 1)
                    for g in range(2):
                        if n * T + i >= 1:
                            pe.wait_ge(S["hT_ready"], 2 * (n * T + i) - 1 + g)
                        for a in range(4):
                            k = 4 * g + a
                            last = nc.tensor.transpose(banks[4 + g][:, a * P:(a + 1) * P], h[:, i % 2, k * P:(k + 1) * P], ident)
                        last.then_inc(S["hT_mm"], 1)

            def rows_mm(bank, name, i, cols=HALF):
                w = ringv[:, w_slot(name)]
                for k in range(KC):
                    last = mm(bank, hT[:, k, tok0[i]:tok0[i] + P], w[:, k, :], start=(k == 0), stop=(k == KC - 1))
                return last

            for j in range(4):
                mod_mm(j)
                if j >= 1:
                    mod_bc(j - 1)
            mod_bc(3)
            turns(0, h_tok)
            pe.wait_ge(S["kv_ctx_in"], 32)
            for a in range(4):
                last = nc.tensor.transpose(banks[6][:, a * P:(a + 1) * P], kctx[:, a * P:(a + 1) * P], ident)
            last.then_inc(S["kctxT_mm"], 1)

            def qk_turn(v):
                pe.wait_ge(S["qk_ready"], v + 1)
                if v >= 2:
                    pe.wait_ge(S["qkT_ready"], v - 1)
                else:
                    pe.wait_ge(S["hT_ready"], 2 * T)
                for a in range(4):
                    last = nc.tensor.transpose(banks[4 + v % 2][:, a * P:(a + 1) * P], qk_tok[:, v % 2, a * P:(a + 1) * P], ident)
                last.then_inc(S["qkT_mm"], 1)

            pe.wait_ge(S["hT_ready"], 2 * T)
            for u in range(3 * T):
                name = ("qa", "ka", "va")[u // T]
                if u % T == 0:
                    w_wait(pe, name)
                if u >= 4:
                    if u - 4 < 2 * T:
                        pe.wait_ge(S["qk_ready"], u - 3)
                    else:
                        pe.wait_ge(S["va_ready"], u - 3 - 2 * T)
                elif u < 4:
                    pe.wait_ge(S["bc_done"], 8)
                rows_mm(banks[u % 4][:, :], name, u % T).then_inc(S["proj_mm"], 1)
                if 1 <= u <= 2 * T:
                    qk_turn(u - 1)

            NU = 8 * (1 + N_CB)

            def scores(u):
                h = u % 8
                lanes = slice(64 * (h % 2), 64 * (h % 2) + 64)
                if u >= 2:
                    pe.wait_ge(S["max_ready"], u - 1)
                else:
                    pe.wait_ge(S["va_ready"], T)
                    pe.wait_ge(S["qkT_ready"], 2 * T)
                    pe.wait_ge(S["kctxT_ready"], 1)
                bank = banks[u % 2]
                if u < 8:
                    last = mm(bank[:, 0:SEQ], qaT[lanes, h // 2, 0:SEQ], kaT[lanes, h // 2, 0:SEQ], start=True, stop=True)
                else:
                    m = u // 8 - 1
                    q = qaT[lanes, h // 2, SEQ + m * P:SEQ + (m + 1) * P]
                    k = kaT[lanes, h // 2, SEQ:TOK].rearrange("p (r c) -> p r c", c=GRID_W)[:, :, BAND_START[m]:BAND_START[m] + BAND_W]
                    mm(bank[:, 0:BAND].rearrange("p (r c) -> p r c", c=BAND_W), q, k, start=True, stop=True)
                    last = mm(bank[:, BAND:KEYS], q, kctxT[lanes, h // 2, :], start=True, stop=True)
                last.then_inc(S["score_mm"], 1)

            def prob_turn(u):
                n = 1 if u < 8 else 3
                pe.wait_ge(S["prob_ready"], u + 1)
                if u >= 2:
                    pe.wait_ge(S["probT_ready"], u - 1)
                for a in range(n):
                    last = nc.tensor.transpose(banks[2 + u % 2][:, a * P:(a + 1) * P], score[:, u % 2, a * P:(a + 1) * P], ident)
                last.then_inc(S["probT_mm"], 1)

            def values(u):
                h = u % 8
                pair = u // 2
                out = banks[4 + pair % 2][64 * (u % 2):64 * (u % 2) + 64, 0:P]
                pe.wait_ge(S["probT_ready"], u + 1)
                if pair >= 2 and u % 2 == 0:
                    pe.wait_ge(S["pv_used"], pair - 1)
                hc = slice(h * D_HA, (h + 1) * D_HA)
                if u < 8:
                    last = mm(out, va0[:, hc], probT[:, u % 2, 0:P], start=True, stop=True)
                else:
                    m = u // 8 - 1
                    if h == 0:
                        pe.wait_ge(S[f"vband_in{m % 2}"], 16 * 8 * (m // 2 + 1))
                    for a in range(3):
                        vals = vband[:, m % 2, a, hc] if a < 2 else vctx[:, hc]
                        last = mm(out, vals, probT[:, u % 2, a * P:(a + 1) * P], start=(a == 0), stop=(a == 2))
                last.then_inc(S["pv_mm"], 1)

            scores(0)
            for u in range(NU):
                if u + 1 < NU:
                    scores(u + 1)
                prob_turn(u)
                if u >= 1:
                    values(u - 1)
            values(NU - 1)
            barrier(pe, 1)

            pe.wait_ge(S["b_in"], 64)
            for i in range(T):
                for k in range(KC):
                    last = mm(banks[7][:, i * 16:(i + 1) * 16], hT[:, k, tok0[i]:tok0[i] + P], w_ab[:, k, :], start=(k == 0), stop=(k == KC - 1))
            last.then_inc(S["ab_mm"], 1)

            def turn_conv(c):
                pe.wait_ge(S["ys_ready"], c + 1)
                if c >= 2:
                    pe.wait_ge(S["tok_ready"], c - 1)
                elif c == 1:
                    pe.wait_ge(S["gc_used"], 1)
                b = 4 + 2 * (c % 2)
                nc.tensor.transpose(banks[b + 1][:, 0:P], ys[:, c % 2, 0:P], ident)
                for i in range(4):
                    o = SEQ + 2 + i * P
                    last = nc.tensor.transpose(banks[b][:, i * P:(i + 1) * P], ys[:, c % 2, o:o + P], ident)
                last.then_inc(S["tok_mm"], 1)

            for c in range(12):
                name = ("qb", "kb", "vb")[c // 4]
                if c % 4 == 0:
                    w_wait(pe, name)
                if c >= 2:
                    pe.wait_ge(S["xc_ready"], c - 1)
                w = ringv[:, w_slot(name), :, (c % 4) * P:(c % 4 + 1) * P]
                for k in range(KC):
                    mm(banks[2 * (c % 2) + 1][:, 0:SEQ], w[:, k, :], hT[:, k, 0:SEQ], start=(k == 0), stop=(k == KC - 1))
                for k in range(KC):
                    last = mm(banks[2 * (c % 2)][:, :], w[:, k, :], hT[:, k, SEQ:TOK], start=(k == 0), stop=(k == KC - 1))
                last.then_inc(S["cm_mm"], 1)
                if c == 0:
                    pe.wait_ge(S["g_ready"], 1)
                    n = T * H_B
                    mm(banks[7][:, 128:128 + 2 * n], ones, gt[:, 0, 0:2 * n], start=True, stop=True)
                    mm(banks[7][:, 128 + 2 * n:128 + 3 * n], upper, gt[:, 0, 0:n], start=True, stop=True)
                    mm(banks[7][:, 128 + 3 * n:128 + 4 * n], lower, gt[:, 0, n:2 * n], start=True, stop=True).then_inc(S["gc_mm"], 1)
                if c >= 1:
                    turn_conv(c - 1)
            turn_conv(11)
            for i in range(T):
                pe.wait_ge(S["rope_done"], i + 1)
                for g in range(2):
                    if i >= 2:
                        pe.wait_ge(S["kqT_ready"], 2 * (i - 2) + g + 1)
                    elif i == 0:
                        pe.wait_ge(S["xc_ready"], 12)
                    for h in range(H_B):
                        o = g * W_B + h * DK
                        last = nc.tensor.transpose(banks[2 * (i % 2) + g][:, h * P:(h + 1) * P], qkv[:, i, o:o + P], ident)
                    last.then_inc(S["kqT_mm"], 1)

            NL = len(LEVELS)
            pe.wait_ge(S["kqT_ready"], 2 * T)
            pe.wait_ge(S["tok_ready"], 12)
            for p in range(T):
                tile = [0 if p == 0 else (p if d == 0 else T - p) for d in range(2)]
                for d in range(2):
                    U, i = unit[d], tile[d]
                    b = 4 * d
                    if p >= 1:
                        pe.wait_ge(S[f"nwt{d}"], p)
                        pe.wait_ge(S[f"os{d}"], 2 * p)
                    for h in range(H_B):
                        col = (d * T + i) * H_B + h
                        last = mm(banks[b][:, h * P:(h + 1) * P], gt[:, 0, col:col + 1].to_broadcast([P, P]), (upper, lower)[d], start=True, stop=True)
                    last.then_inc(S[f"row_mm{d}"], 1)
                    kd, qd = kdT[:, :, tok0[i]:tok0[i] + P], qdT[:, :, tok0[i]:tok0[i] + P]
                    for h in range(H_B):
                        mm(banks[b + 1][:, h * P:(h + 1) * P], kd[:, h], kd[:, h], start=True, stop=True)
                        last = mm(banks[b + 2][:, h * P:(h + 1) * P], kd[:, h], qd[:, h], start=True, stop=True)
                    last.then_inc(S[f"kq_mm{d}"], 1)
                for n in range(NL):
                    for d in range(2):
                        U = unit[d]
                        b = 4 * d
                        if n == 0:
                            pe.wait_ge(S[f"dpre{d}"], p + 1)
                            pe.wait_ge(S[f"prep{d}"], 2 * p + 1)
                            pe.wait_ge(S[f"bt{d}"], 2 * p + 2)
                        else:
                            pe.wait_ge(S[f"mn{d}"], NL * p + n)
                        pe.wait_ge(S[f"msk{d}"], NL * p + n + 1)
                        for h in range(H_B):
                            last = mm(banks[b][:, h * P:(h + 1) * P], U[f"mask{n % 2}"][:, h], U["inv"][:, h], start=True, stop=True)
                        last.then_inc(S[f"x_mm{d}"], 1)
                    for d in range(2):
                        U = unit[d]
                        b = 4 * d
                        pe.wait_ge(S[f"xs{d}"], NL * p + n + 1)
                        for h in range(H_B):
                            mm(banks[b + 1][:, h * P:(h + 1) * P], U["invT"][:, h], U["xs"][:, h], start=True, stop=True)
                            last = mm(banks[b + 2][:, h * P:(h + 1) * P], U["xs"][:, h], U["invT"][:, h], start=True, stop=True)
                        last.then_inc(S[f"p_mm{d}"], 1)
                for d in range(2):
                    U = unit[d]
                    pe.wait_ge(S[f"mn{d}"], NL * (p + 1))
                    pe.wait_ge(S[f"prep{d}"], 2 * p + 2)
                    for h in range(H_B):
                        last = mm(banks[4 * d][:, h * P:(h + 1) * P], U["kexp"][:, h], U["invT"][:, h], start=True, stop=True)
                    last.then_inc(S[f"wt_mm{d}"], 1)
                for d in range(2):
                    U, i = unit[d], tile[d]
                    pe.wait_ge(S[f"nwt{d}"], p + 1)
                    if p == 1:
                        pe.wait_ge(S["states_in"], 64)
                    if p == 0:
                        pe.wait_ge(S[f"st{d}"], 1)
                    else:
                        pe.wait_ge(S[f"os{d}"], 2 * p)
                    for h in range(H_B):
                        out = banks[4 * d + 1][:, h * P:(h + 1) * P]
                        mm(out, U["invT"][:, h], qkv[:, i, 2 * W_B + h * P:2 * W_B + (h + 1) * P], start=True, stop=False)
                        last = mm(out, U["nwT"][:, h], U["state"][:, h], start=False, stop=True)
                    last.then_inc(S[f"vn_mm{d}"], 1)
                for d in range(2):
                    U = unit[d]
                    pe.wait_ge(S[f"vn{d}"], p + 1)
                    for h in range(H_B):
                        out = banks[4 * d + 3][:, h * P:(h + 1) * P]
                        mm(out, U["erow"][:, h], U["state"][:, h], start=True, stop=False)
                        last = mm(out, U["intraT"][:, h], U["vnew"][:, h], start=False, stop=True)
                    last.then_inc(S[f"o_mm{d}"], 1)
                    for h in range(H_B):
                        last = mm(banks[4 * d + 2][:, h * P:(h + 1) * P], U["kend"][:, h], U["vnew"][:, h], start=True, stop=True)
                    last.then_inc(S[f"o_mm{d}"], 1)
            barrier(pe, 2)

            def turn_ob(i):
                pe.wait_ge(S["ob_ready"], i + 1)
                if i >= 2:
                    pe.wait_ge(S["obT_ready"], i - 1)
                for a in range(4):
                    last = nc.tensor.transpose(banks[4 + i % 2][:, a * P:(a + 1) * P], o_acc[:, i, a * P:(a + 1) * P], ident)
                last.then_inc(S["obT_mm"], 1)

            w_wait(pe, "zb")
            for i in range(T):
                if i >= 2:
                    pe.wait_ge(S["zs_ready"], i - 1)
                rows_mm(banks[i % 2][:, :], "zb", i).then_inc(S["z_mm"], 1)
                if i >= 1:
                    turn_ob(i - 1)
            turn_ob(T - 1)
            pe.wait_ge(S["zs_ready"], T)
            for j in range(4, 12):
                mod_mm(j)
                if j >= 5:
                    mod_bc(j - 1)
            mod_bc(11)
            pe.wait_ge(S["obT_ready"], T)
            pe.wait_ge(S["bc_done"], 24)
            for u in range(NHALF * T):
                n, i = u // T, u % T
                b = 4 * (u % 2)
                if i == 0:
                    for name in (f"proj{n}", f"ga{n}", f"gb{n}"):
                        w_wait(pe, name)
                if u >= 2:
                    pe.wait_ge(S["merged_ready"], u - 1)
                w = ringv[:, w_slot(f"proj{n}")]
                for k in range(4):
                    mm(banks[b][:, :], oaT[:, k, tok0[i]:tok0[i] + P], w[:, k, :], start=(k == 0), stop=(k == 3))
                for k in range(4):
                    mm(banks[b + 1][:, :], obT[:, k, tok0[i]:tok0[i] + P], w[:, 4 + k, :], start=(k == 0), stop=(k == 3))
                rows_mm(banks[b + 2][:, :], f"ga{n}", i)
                rows_mm(banks[b + 3][:, :], f"gb{n}", i).then_inc(S["merge_mm"], 1)
            pe.wait_ge(S["merged_ready"], NHALF * T)
            for i in range(T):
                for g in range(2):
                    if i >= 1:
                        pe.wait_ge(S["mT_ready"], 2 * i - 1 + g)
                    for a in range(4):
                        k = 4 * g + a
                        last = nc.tensor.transpose(banks[4 + g][:, a * P:(a + 1) * P], merged[:, i, k * P:(k + 1) * P], ident)
                    last.then_inc(S["mT_mm"], 1)
            pe.wait_ge(S["mT_ready"], 2 * T)
            for u in range(NHALF * T):
                n, i = u // T, u % T
                if i == 0:
                    w_wait(pe, f"out{n}")
                if u >= 4:
                    pe.wait_ge(S["x2_ready"], u - 3)
                rows_mm(banks[u % 4][:, :], f"out{n}", i).then_inc(S["out_mm"], 1)
            turns(1, h2_tok)
            pe.wait_ge(S["hT_ready"], 4 * T)
            pe.wait_ge(S["b_in"], 112)
            pe.wait_ge(S["x2_ready"], NHALF * T)
            for i in range(T):
                for k in range(KC):
                    last = mm(banks[0][:, i * 36:(i + 1) * 36], hT[:, k, tok0[i]:tok0[i] + P], w_router[:, k, :], start=(k == 0), stop=(k == KC - 1))
            last.then_inc(S["logit_mm"], 1)
            pe.wait_ge(S["chosen_ready"], 1)
            for i in range(T):
                for j in range(i):
                    mm(banks[1][:, i * N_EXPERTS:(i + 1) * N_EXPERTS], ones, picked[:, j, :], start=(j == 0), stop=False)
                mm(banks[1][:, i * N_EXPERTS:(i + 1) * N_EXPERTS], earlier, picked[:, i, :], start=(i == 0), stop=True)
            for i in range(T):
                last = mm(banks[1][:, T * N_EXPERTS:(T + 1) * N_EXPERTS], ones, picked[:, i, :], start=(i == 0), stop=(i == T - 1))
            last.then_inc(S["place_mm"], 1)
            barrier(pe, 3)

            is_dense = pe.value_load(dense[0:1, 0:1])
            with pe.If(is_dense > 0):
                def turn_hid(u):
                    pe.wait_ge(S["hid_ready"], u + 1)
                    if u >= 2:
                        pe.wait_ge(S["hidT_ready"], u - 1)
                    for a in range(2):
                        last = nc.tensor.transpose(banks[2 + u % 2][:, a * P:(a + 1) * P], hid[:, u % 2, a * P:(a + 1) * P], ident)
                    last.then_inc(S["hidT_mm"], 1)

                def down(u):
                    e = u // T
                    pe.wait_ge(S["hidT_ready"], u + 1)
                    b = 4 + 2 * (u % 2)
                    if u >= 2:
                        pe.wait_ge(S["acc_done"], u - 1)
                    for n in range(NHALF):
                        for k in range(2):
                            last = mm(banks[b + n][:, :], hidT[:, u % 2, k * P:(k + 1) * P], edown[e % 3][:, k, n * HALF:(n + 1) * HALF],
                                      start=(k == 0), stop=(k == 1))
                    last.then_inc(S["down_mm"], 1)

                for u in range(N_EXPERTS * T):
                    e, i = u // T, u % T
                    if i == 0:
                        pe.wait_ge(S[f"w_in{e % 3}"], expert_loaded(e))
                    if u >= 2:
                        pe.wait_ge(S["hid_ready"], u - 1)
                    for k in range(KC):
                        last = mm(banks[u % 2][:, :], hT[:, k, tok0[i]:tok0[i] + P], eup[e % 3][:, k, :], start=(k == 0), stop=(k == KC - 1))
                    last.then_inc(S["eup_mm"], 1)
                    if u >= 1:
                        turn_hid(u - 1)
                        if u >= 2:
                            down(u - 2)
                turn_hid(N_EXPERTS * T - 1)
                down(N_EXPERTS * T - 2)
                down(N_EXPERTS * T - 1)
            with pe.Else():
                def turn_rows(e):
                    pe.wait_ge(S[f"rows_in{e % 4}"], 16 * (e // 4 + 1))
                    if e >= 1:
                        pe.wait_ge(S["rowsT_ready"], e)
                        pe.wait_ge(S["rowsT_ready2"], e)
                    for g in range(2):
                        for a in range(4):
                            k = 4 * g + a
                            last = nc.tensor.transpose(banks[g][:, a * P:(a + 1) * P], rows_in[e % 4][:, k * P:(k + 1) * P], ident)
                        last.then_inc(S["rowsT_mm"], 1)

                def up(e):
                    pe.wait_ge(S[f"w_in{e % 3}"], expert_loaded(e))
                    pe.wait_ge(S["rowsT_ready"], e + 1)
                    pe.wait_ge(S["rowsT_ready2"], e + 1)
                    if e >= 2:
                        pe.wait_ge(S["hid_ready"], e - 1)
                    for k in range(KC):
                        last = mm(banks[2 + e % 2][:, :], rowsT[e % 2][:, k, :], eup[e % 3][:, k, :], start=(k == 0), stop=(k == KC - 1))
                    last.then_inc(S["eup_mm"], 1)

                def turn_hidden(e):
                    pe.wait_ge(S["hid_ready"], e + 1)
                    if e >= 2:
                        pe.wait_ge(S["hidT_ready"], e - 1)
                    for a in range(2):
                        last = nc.tensor.transpose(banks[4 + e % 2][:, a * P:(a + 1) * P], hid[:, e % 2, a * P:(a + 1) * P], ident)
                    last.then_inc(S["hidT_mm"], 1)

                def down_rows(e):
                    pe.wait_ge(S["hidT_ready"], e + 1)
                    if e >= 1:
                        pe.wait_ge(S["acc_done"], e)
                        pe.wait_ge(S["s_out2"], e)
                    for n in range(NHALF):
                        for k in range(2):
                            last = mm(banks[6 + n][:, :], hidT[:, e % 2, k * P:(k + 1) * P], edown[e % 3][:, k, n * HALF:(n + 1) * HALF],
                                      start=(k == 0), stop=(k == 1))
                    last.then_inc(S["down_mm"], 1)

                turn_rows(0)
                for e in range(N_EXPERTS):
                    up(e)
                    if e + 1 < N_EXPERTS:
                        turn_rows(e + 1)
                    if e >= 1:
                        down_rows(e - 1)
                    turn_hidden(e)
                down_rows(N_EXPERTS - 1)


_OUTS = [("y", (T, P, D)), ("new_k", (P, W_A)), ("new_v", (P, W_A)), ("new_state", (2, P, H_B, P))]


def layout(i):
    f = {k: np.asarray(v) for k, v in i.items()}

    def blocked(w, cols=HALF):
        k, n = w.shape
        return w.reshape(k // P, P, n // cols, cols).transpose(2, 1, 0, 3).reshape(n // cols, P, -1)

    a = {}
    a["x"] = np.concatenate([f["x_prompt"][0], f["x_sample"][0]]).reshape(T, P, D)
    a["cT"] = np.stack([f["c_ctx"], f["c"][0]], axis=1).reshape(KC, P, 2).transpose(1, 0, 2).reshape(P, -1)
    wi = f["w_in"][0]
    mod, win = blocked(f["w_mod"][0]), blocked(np.concatenate([wi[:, :3584], wi[:, 3600:]], axis=1))
    proj = blocked(np.concatenate([f["w_proj_a"][0], f["w_proj_b"][0]], axis=0))
    out = blocked(f["w_out"][0])
    by_name = {f"mod{j}": mod[j] for j in range(12)}
    for n, name in enumerate(["qa", "ka", "va", "qb", "kb", "vb", "zb", "ga0", "ga1", "gb0", "gb1"]):
        by_name[name] = win[n]
    for n in range(2):
        by_name[f"proj{n}"], by_name[f"out{n}"] = proj[n], out[n]
    a["w_blocks"] = np.stack([by_name[name] for name in BLOCKS])
    a["w_ab"] = blocked(wi[:, 3584:3600], 16)[0]
    a["bmod"] = np.broadcast_to(f["b_mod"].reshape(1, 12, HALF), (2, 12, HALF))
    a["norm_w"] = np.broadcast_to(np.stack([f["norm1_w"][0], f["norm2_w"][0]])[None], (2, 2, D))
    row = np.concatenate([f["q_norm_w"][0], f["k_norm_w"][0], f["o_norm_w"][0], f["b_router_g"][0], f["b_router_e"][0],
                          f["dt_bias"][0].reshape(-1), f["a_log"][0].reshape(-1), np.arange(EXP_PER_GROUP, 0, -1, dtype=np.float32), np.arange(N_EXPERTS, dtype=np.float32)])
    a["rows"] = np.broadcast_to(row, (P, R_ALL))
    a["conv_w"] = f["conv_w"][0].reshape(CONV_K, 12, P).transpose(2, 1, 0).reshape(P, -1)
    a["w_router"] = blocked(np.concatenate([f["w_router_g"][0], f["w_router_e"][0]], axis=1), 36)[0]
    a["w_up"] = np.stack([blocked(np.concatenate([f["w_exp_gate"][0, e], f["w_exp_up"][0, e]], axis=1))[0] for e in range(N_EXPERTS)])
    a["w_down"] = np.stack([blocked(f["w_exp_down"][0, e], D)[0] for e in range(N_EXPERTS)])
    a["kctx"] = f["cache_attn_k"].reshape(P, W_A)
    a["vctx"] = f["cache_attn_v"].reshape(P, W_A)
    a["state0"] = np.stack([f["state_delta_fwd"][0, 0], f["state_delta_bwd"][0, 0]]).transpose(0, 2, 1, 3).reshape(2, P, -1)
    rpb = f["rpb"][0]
    r, q, kr, k = (x.reshape(s) for x, s in ((np.arange(ROWS), (-1, 1, 1, 1)), (np.arange(QB_W), (1, -1, 1, 1)),
                                             (np.arange(ROWS), (1, 1, -1, 1)), (np.arange(BAND_W), (1, 1, 1, -1))))
    bias = np.zeros((3, P, H_A, KEYS), rpb.dtype)
    for m in (0, 1, 3):
        q_col, k_col = m * QB_W + q, BAND_START[m] + k
        start = np.clip(q_col - WIN_W // 2, 0, GRID_W - WIN_W)
        seen = (k_col >= start) & (k_col < start + WIN_W) & (kr >= 0) & (r >= 0)
        at = rpb[:, kr - r + WIN_H - 1 + 0 * q + 0 * k, np.clip(k_col - q_col + WIN_W - 1, 0, 2 * WIN_W - 2) + 0 * kr + 0 * r]
        at = np.where(seen[None], at, np.float32(-BIG))
        bias[BIAS_OF[m], :, :, :BAND] = at.reshape(H_A, P, BAND).transpose(1, 0, 2)
    a["bias"] = bias.reshape(3, P, -1)
    tok = np.arange(TOK).reshape(T, P).T
    a["payload"] = np.stack([np.stack([tok, tok + r * TOK], axis=2) for r in range(2)], axis=1).reshape(P, -1).astype(np.int32)
    a["const"], a["level_mask"] = constants()
    pos = np.arange(DEC_SEQ)
    inv = 10000.0 ** (-np.arange(DK // 4, dtype=np.float32) / (DK // 4))
    ang = np.concatenate([(pos // GRID_W)[:, None] * inv, (pos % GRID_W)[:, None] * inv], axis=1).astype(np.float32)
    a["rope"] = np.stack([np.cos(ang), np.sin(ang)], axis=1).reshape(4, P, 2, 64).transpose(1, 0, 2, 3).reshape(P, -1).astype(np.float32)
    return a


def kernel(**inputs):
    import concourse.bacc as bacc
    from concourse.bass_utils import run_bass_kernel_spmd

    nc = bacc.Bacc("TRN2", target_bir_lowering=False, num_devices=1)
    arrays, t = {}, {}
    for name, a in layout(inputs).items():
        if name == "level_mask":
            a = a.astype(mybir.dt.np(BF16))
        a = np.ascontiguousarray(a)
        arrays[f"in_{name}"] = a
        t[name] = nc.dram_tensor(f"in_{name}", a.shape, mybir.dt.from_np(a.dtype), kind="ExternalInput").ap()
    for name, shape in _OUTS:
        t[name] = nc.dram_tensor(f"out_{name}", shape, F32, kind="ExternalOutput").ap()
    t["v_scratch"] = nc.dram_tensor("v_scratch", (T - 1, P, W_A), F32, kind="Internal").ap()
    t["h_scratch"] = nc.dram_tensor("h_scratch", (TOK, D), F32, kind="Internal").ap()
    t["y_scratch"] = nc.dram_tensor("y_scratch", (2 * TOK, D), F32, kind="Internal").ap()
    t["slot_table"] = nc.dram_tensor("slot_table", (CAP * N_EXPERTS, 2), I32, kind="Internal").ap()
    build(nc, t)
    r = run_bass_kernel_spmd(nc, [arrays], core_ids=[0]).results[0]
    y = r["out_y"].reshape(TOK, D)
    state = r["out_new_state"].transpose(0, 2, 1, 3).reshape(2, 1, 1, H_B, DK, DK)
    return (y[:SEQ].reshape(1, SEQ, D), y[SEQ:].reshape(1, DEC_SEQ, D), r["out_new_k"].reshape(1, 1, SEQ, H_A, D_HA),
            r["out_new_v"].reshape(1, 1, SEQ, H_A, D_HA), state[0], state[1])
```
